# Optimizing a Trainium2 kernel written in Bass

```python
import math
import jax, jax.numpy as jnp
from jax import lax
import numpy as np

D_MODEL = 1024
BATCH = 1
SEQ = 1024
DEPTH = 1
DEC_BATCH = 8
DEC_SEQ = 8
PAST_LEN = 8192
PAGE_SIZE = 128

D_MIX = D_MODEL
POOL_WIDTH = D_MIX // 2
POOL_WINDOWS = (2, 4, 8, 16)
N_POOL_GROUPS = len(POOL_WINDOWS)
POOL_GROUP = POOL_WIDTH // N_POOL_GROUPS
POOL_BUF = max(POOL_WINDOWS) - 1
GLA_WIDTH = D_MIX - POOL_WIDTH
GLA_HEADS = 4
GLA_HEAD_V = GLA_WIDTH // GLA_HEADS
GLA_HEAD_K = GLA_HEAD_V // 2
GLA_KEY = GLA_HEADS * GLA_HEAD_K
GLA_GATE_RANK = 16
GLA_GATE_NORM = 16.0
GLA_CHUNK = 64
IN_SIZES = (POOL_WIDTH, GLA_KEY, GLA_KEY, GLA_WIDTH, GLA_GATE_RANK, GLA_WIDTH)
D_IN = sum(IN_SIZES)
D_FF = 2816
N_ADA = 9
EPS = 1e-6

kernel_name = "hymba_pool_gla_macaron_adaln_step"

def rms_norm(x, g):
    x32 = x.astype(jnp.float32)
    y = x32 * lax.rsqrt(jnp.mean(x32 * x32, axis=-1, keepdims=True) + EPS)
    return (y * g.astype(jnp.float32)).astype(x.dtype)

def modulate(h, shift, scale):
    return h * (1 + scale) + shift

def swiglu(h, w_up, w_down):
    g, u = jnp.split(h @ w_up, 2, axis=-1)
    return (jax.nn.silu(g) * u) @ w_down

def split_in(proj):
    outs, off = [], 0
    for s in IN_SIZES:
        outs.append(proj[..., off:off + s])
        off += s
    return outs

def pool_mixer(u, buf, pos0, w_pool, pool_scale):
    B, T, P = u.shape
    ext = jnp.concatenate([buf.astype(u.dtype), u], axis=1).astype(jnp.float32)
    cs = jnp.concatenate([jnp.zeros((B, 1, P), jnp.float32), jnp.cumsum(ext, axis=1)], axis=1)
    pos = pos0 + jnp.arange(T, dtype=jnp.int32)
    cur = ext[:, POOL_BUF:, :]
    outs = []
    for g, w in enumerate(POOL_WINDOWS):
        lo, hi = g * POOL_GROUP, (g + 1) * POOL_GROUP
        win = cs[:, POOL_BUF + 1:POOL_BUF + 1 + T, lo:hi] - cs[:, POOL_BUF + 1 - w:POOL_BUF + 1 - w + T, lo:hi]
        cnt = jnp.minimum(pos + 1, w).astype(jnp.float32)[None, :, None]
        p = win / cnt - cur[:, :, lo:hi]
        outs.append(p @ w_pool[g].astype(jnp.float32))
    z = jnp.concatenate(outs, axis=-1) * pool_scale.astype(jnp.float32)
    new_buf = ext[:, -POOL_BUF:, :]
    return z.astype(u.dtype), new_buf

def gla_mixer(q, k, v, log_a, S0):
    B, T, H, dk = q.shape
    C = math.gcd(T, GLA_CHUNK)
    N = T // C

    def blk(t):
        return t.reshape(B, N, C, H, t.shape[-1]).transpose(0, 3, 1, 2, 4)

    q, k, v, log_a = blk(q), blk(k), blk(v), blk(log_a)
    b = jnp.cumsum(log_a, axis=3)
    b_last = b[:, :, :, -1:, :]
    q_in = q * jnp.exp(b) * (dk ** -0.5)
    k_in = k * jnp.exp(-b)
    k_dec = k * jnp.exp(b_last - b)
    mask = jnp.tril(jnp.ones((C, C), dtype=bool))
    att = jnp.where(mask, jnp.einsum('bhncd,bhnsd->bhncs', q_in, k_in), 0.0)
    o = jnp.einsum('bhncs,bhnse->bhnce', att, v)
    upd = jnp.einsum('bhnsd,bhnse->bhnde', k_dec, v)
    decay = jnp.exp(b_last[:, :, :, 0, :])

    def step(S, xs):
        dec, u = xs
        return dec[..., None] * S + u, S

    S_fin, S_prev = lax.scan(step, S0, (jnp.moveaxis(decay, 2, 0), jnp.moveaxis(upd, 2, 0)))
    S_prev = jnp.moveaxis(S_prev, 0, 2)
    o = o + jnp.einsum('bhncd,bhnde->bhnce', q_in, S_prev)
    o = o.transpose(0, 2, 3, 1, 4).reshape(B, T, H, v.shape[-1])
    return o, S_fin

def layer(x, c, pool_buf, gla_S, pos0, ln1, ln_mix, ln2, w_ada, b_ada, w_f1_up, w_f1_down,
          w_in, w_gk2, b_gk2, w_pool, pool_scale, gla_norm, w_out, w_f2_up, w_f2_down):
    B, T, _ = x.shape
    ada = jax.nn.silu(c) @ w_ada + b_ada
    sh1, sc1, g1, shm, scm, gm, sh2, sc2, g2 = [a[:, None, :] for a in jnp.split(ada, N_ADA, axis=-1)]
    h = modulate(rms_norm(x, ln1), sh1, sc1)
    x = x + 0.5 * g1 * swiglu(h, w_f1_up, w_f1_down)
    h = modulate(rms_norm(x, ln_mix), shm, scm)
    u, q, k, v, glr, og = split_in(h @ w_in)
    z_pool, new_buf = pool_mixer(u, pool_buf, pos0, w_pool, pool_scale)
    log_a = jax.nn.log_sigmoid((glr @ w_gk2 + b_gk2).astype(jnp.float32)) / GLA_GATE_NORM
    f32 = jnp.float32
    o, S_new = gla_mixer(q.reshape(B, T, GLA_HEADS, GLA_HEAD_K).astype(f32),
                         k.reshape(B, T, GLA_HEADS, GLA_HEAD_K).astype(f32),
                         v.reshape(B, T, GLA_HEADS, GLA_HEAD_V).astype(f32),
                         log_a.reshape(B, T, GLA_HEADS, GLA_HEAD_K),
                         gla_S.astype(f32))
    o = rms_norm(o, gla_norm).reshape(B, T, GLA_WIDTH) * jax.nn.silu(og.astype(f32))
    mix = jnp.concatenate([z_pool, o.astype(x.dtype)], axis=-1) @ w_out
    x = x + gm * mix
    h = modulate(rms_norm(x, ln2), sh2, sc2)
    x = x + 0.5 * g2 * swiglu(h, w_f2_up, w_f2_down)
    return x, new_buf.astype(x.dtype), S_new.astype(x.dtype)

def setup_inputs(seed: int = 0) -> dict:
    key = jax.random.key(seed)
    ks = jax.random.split(key, 24)

    def nrm(k, shape, scale=1.0):
        return jax.random.normal(k, shape, jnp.float32) * scale

    return {
        "x_prompt": nrm(ks[0], (BATCH, SEQ, D_MODEL)),
        "x_sample": nrm(ks[1], (DEC_BATCH, DEC_SEQ, D_MODEL)),
        "state_pool": nrm(ks[2], (DEPTH, DEC_BATCH, POOL_BUF, POOL_WIDTH)),
        "state_gla": nrm(ks[3], (DEPTH, DEC_BATCH, GLA_HEADS, GLA_HEAD_K, GLA_HEAD_V), 0.5),
        "c_prompt": nrm(ks[4], (BATCH, D_MODEL)),
        "c_sample": nrm(ks[5], (DEC_BATCH, D_MODEL)),
        "ln_ffn1": 1.0 + nrm(ks[6], (DEPTH, D_MODEL), 0.05),
        "ln_mix": 1.0 + nrm(ks[7], (DEPTH, D_MODEL), 0.05),
        "ln_ffn2": 1.0 + nrm(ks[8], (DEPTH, D_MODEL), 0.05),
        "w_ada": nrm(ks[9], (DEPTH, D_MODEL, N_ADA * D_MODEL), 0.5 * D_MODEL ** -0.5),
        "b_ada": nrm(ks[10], (DEPTH, N_ADA * D_MODEL), 0.01),
        "w_ffn1_up": nrm(ks[11], (DEPTH, D_MODEL, 2 * D_FF), D_MODEL ** -0.5),
        "w_ffn1_down": nrm(ks[12], (DEPTH, D_FF, D_MODEL), D_FF ** -0.5),
        "w_in": nrm(ks[13], (DEPTH, D_MODEL, D_IN), D_MODEL ** -0.5),
        "w_gk2": nrm(ks[14], (DEPTH, GLA_GATE_RANK, GLA_KEY), GLA_GATE_RANK ** -0.5),
        "b_gk2": nrm(ks[15], (DEPTH, GLA_KEY), 0.1),
        "w_pool": nrm(ks[16], (DEPTH, N_POOL_GROUPS, POOL_GROUP, POOL_GROUP), POOL_GROUP ** -0.5),
        "pool_scale": 1.0 + nrm(ks[17], (DEPTH, POOL_WIDTH), 0.1),
        "gla_norm": 1.0 + nrm(ks[18], (DEPTH, GLA_HEAD_V), 0.05),
        "w_out": nrm(ks[19], (DEPTH, D_MIX, D_MODEL), D_MIX ** -0.5),
        "w_ffn2_up": nrm(ks[20], (DEPTH, D_MODEL, 2 * D_FF), D_MODEL ** -0.5),
        "w_ffn2_down": nrm(ks[21], (DEPTH, D_FF, D_MODEL), D_FF ** -0.5),
        "ln_final": 1.0 + nrm(ks[22], (D_MODEL,), 0.05),
    }

def reference(x_prompt, x_sample, state_pool, state_gla, c_prompt, c_sample,
              ln_ffn1, ln_mix, ln_ffn2, w_ada, b_ada, w_ffn1_up, w_ffn1_down,
              w_in, w_gk2, b_gk2, w_pool, pool_scale, gla_norm, w_out,
              w_ffn2_up, w_ffn2_down, ln_final):
    bp = x_prompt.shape[0]
    xp, xs = x_prompt, x_sample
    pool_p, gla_p, pool_s, gla_s = [], [], [], []
    for l in range(DEPTH):
        w = (ln_ffn1[l], ln_mix[l], ln_ffn2[l], w_ada[l], b_ada[l], w_ffn1_up[l], w_ffn1_down[l],
             w_in[l], w_gk2[l], b_gk2[l], w_pool[l], pool_scale[l], gla_norm[l], w_out[l],
             w_ffn2_up[l], w_ffn2_down[l])
        buf0 = jnp.zeros((bp, POOL_BUF, POOL_WIDTH), xp.dtype)
        S0 = jnp.zeros((bp, GLA_HEADS, GLA_HEAD_K, GLA_HEAD_V), jnp.float32)
        xp, nb_p, ns_p = layer(xp, c_prompt, buf0, S0, 0, *w)
        xs, nb_s, ns_s = layer(xs, c_sample, state_pool[l], state_gla[l], PAST_LEN, *w)
        pool_p.append(nb_p); gla_p.append(ns_p); pool_s.append(nb_s); gla_s.append(ns_s)
    y_prompt = rms_norm(xp, ln_final)
    y_sample = rms_norm(xs, ln_final)
    new_pool_prompt = jnp.stack(pool_p)
    new_gla_prompt = jnp.stack(gla_p)
    new_pool_sample = jnp.stack(pool_s)
    new_gla_sample = jnp.stack(gla_s)
    return (y_prompt, y_sample, new_pool_prompt, new_gla_prompt, new_pool_sample, new_gla_sample)


_drawn_inputs = setup_inputs


def setup_inputs(seed=0):
    import zlib

    import numpy as np

    out = dict(_drawn_inputs(seed))
    spreads = {}
    factors = {'ln_ffn1': 5.772, 'ln_ffn2': 8.0, 'pool_scale': 9.245, 'gla_norm': 25.813}
    for name, (base, spread) in spreads.items():
        noise = np.random.default_rng([zlib.crc32(name.encode()), seed]).standard_normal(out[name].shape)
        drawn = base * np.exp(spread * noise) if base else spread * noise
        out[name] = __import__('jax').numpy.asarray(drawn.astype(out[name].dtype))
    for name, factor in factors.items():
        out[name] = (out[name] * factor).astype(out[name].dtype)
    return out
```

```python
from contextlib import ExitStack

import numpy as np

import concourse.bass as bass
from concourse import mybir

F32 = mybir.dt.float32
F32R = mybir.dt.float32r
U32 = mybir.dt.uint32
ALU = mybir.AluOpType
ACT = mybir.ActivationFunctionType

P = 128
D = 1024
KT = D // P
SEQ = 1024
NSEQ, TSEQ = 8, 8
NS = NSEQ * TSEQ
TOK = SEQ + NS
F = 2816
NF = F // P
FB = 2
NB = NF // FB
CH0 = (0, 384, 768)
CHN = (384, 384, 320)
NC = 3
CMAX = 384
LASTP = CHN[2] - NS
HEADS, DK, DV = 4, 64, 128
GC = 64
PW = (2, 4, 8, 16)
HALO = 15
EW = HALO + LASTP + NSEQ * (HALO + TSEQ)
SB = HALO + LASTP
SW = HALO + TSEQ
EPS = 1e-6
NADA = 9
AU = 512
NAU = NADA * D // AU
AU_FIRST = NAU - NB
V_U, V_Q, V_K, V_V, V_GLR, V_OG = 0, 512, 768, 1024, 1536, 1552

PROJ = ([("glr", 0, V_GLR)] + [("k", j, V_K + P * j) for j in range(2)] + [("q", j, V_Q + P * j) for j in range(2)]
        + [("v", j, V_V + P * j) for j in range(4)] + [("u", j, V_U + P * j) for j in range(4)]
        + [("og", j, V_OG + P * j) for j in range(4)])
NPROJ = len(PROJ)
UPC = NPROJ + KT
IDX = {(kind, j): i for i, (kind, j, _) in enumerate(PROJ)}
RING = 6
W_F1, W_MIX, W_F2 = 0, NB * 6, NB * 6 + NC * UPC
NWS = 3
PAIRS = (3, 3, 2)

R_BADA, R_LN1, R_LNM, R_LN2, R_BGK, R_PS, R_GN, R_END = 0, 72, 80, 88, 96, 98, 102, 103
C_ID, C_RM, C_RATIO, C_CM, C_SM, C_SEQ, C_SEL, C_END = 0, 128, 576, 636, 700, 764, 772, 782


def constants():
    c = np.zeros((P, C_END), np.float32)
    c[:, C_ID:C_ID + P] = np.eye(P)
    c[:, C_RM:C_RM + CMAX] = (np.arange(CMAX) % GC != 0)
    c[:, C_RM + CMAX:C_RM + CMAX + NS] = (np.arange(NS) % TSEQ != 0)
    for g, w in enumerate(PW):
        c[:, C_RATIO + HALO * g:C_RATIO + HALO * (g + 1)] = w / np.minimum(np.arange(HALO) + 1, w)
    s, t = np.arange(P)[:, None] % GC, np.arange(GC)[None]
    c[:, C_CM:C_CM + GC] = s <= t
    c[:, C_SM:C_SM + GC] = (s <= t) & (s // TSEQ == t // TSEQ)
    c[:, C_SEQ:C_SEQ + NSEQ] = s // TSEQ == np.arange(NSEQ)[None]
    c[:, C_SEL:C_SEL + 10] = np.arange(P)[:, None] % 32 == np.arange(10)[None]
    return c


class Steps:

    def __init__(self, eng, sem):
        self.eng, self.sem, self.n, self.base, self.start = eng, sem, 0, None, 0

    def loop(self, i, per):
        self.base, self.start, self.per = i * per, self.n, per

    def end_loop(self, trips):
        assert self.n - self.start == self.per, (self.n - self.start, self.per)
        self.n = self.start + self.per * trips
        self.base = None

    def __call__(self, ins):
        self.n += 1
        ins.then_inc(self.sem, 1)
        self.eng.wait_ge(self.sem, self.n if self.base is None else self.base + self.n)


def program(nc, i, o):
    es = ExitStack()

    def sem(name):
        return es.enter_context(nc.semaphore(name))

    def sb(name, shape, dt=F32, ctx=es):
        return ctx.enter_context(nc.sbuf_tensor(name, shape, dt))

    with es:
        xT = sb("xT", [P, KT, TOK])
        hh = sb("hh", [P, KT, TOK], F32R)
        hl = sb("hl", [P, KT, TOK], F32R)
        ws = sb("ws", [P, NWS, 1024])
        tmp = sb("tmp", [P, 8 * CMAX])
        cst = sb("cst", [P, C_END])
        ones = sb("ones", [P, P])
        vec = sb("vec", [P, R_END + 1])
        ada = sb("ada", [P, NADA * KT, 9])
        coef = sb("coef", [P, 3, KT, 9])

        def tb(k):
            return tmp[:, k * CMAX:(k + 1) * CMAX]

        with ExitStack() as ffn:
            wh = sb("wh", [P, 6, 1024], F32R, ffn)
            wl = sb("wl", [P, 6, 1024], F32R, ffn)
            ah = sb("ah", [P, FB, TOK], F32R, ffn)
            al = sb("al", [P, FB, TOK], F32R, ffn)
            with ExitStack() as first:
                aws = sb("aws", [P, 2, AU], F32, first)
                csT = sb("csT", [P, KT, 32], F32, first)
                aev = sb("aev", [P, AU], F32, first)
            with ExitStack() as last:
                lnf = sb("lnf", [P, D], F32, last)
                rsf = sb("rsf", [P, 9, 8], F32, last)
        with ExitStack() as start:
            xin = sb("xin", [P, 9, D], F32, start)
            vin = sb("vin", [R_END, P], F32, start)
            cin = sb("cin", [9, D], F32, start)
        with ExitStack() as end:
            yst = sb("yst", [P, 2, D], F32, end)
        with ExitStack() as mix:
            qs = sb("qs", [P, 2, CMAX], F32, mix)
            ks = sb("ks", [P, 2, CMAX], F32, mix)
            bs = sb("bs", [P, 2, CMAX], F32, mix)
            t1 = sb("t1", [P, 2, CMAX], F32, mix)
            vs = sb("vs", [P, 3, 512], F32, mix)
            og = sb("og", [P, 4, CMAX], F32, mix)
            E = sb("E", [P, 4, EW], F32, mix)
            attS = sb("attS", [P, 4, P], F32, mix)
            S = sb("S", [P, 3, 2, DV], F32, mix)
            S0 = sb("S0", [P, 2, NSEQ, DV], F32, mix)
            mwh = sb("mwh", [P, 2, 1024], F32R, mix)
            mwl = sb("mwl", [P, 2, 1024], F32R, mix)
            kdT = sb("kdT", [P, 2 * P], F32, mix)
            rows = sb("rows", [P, 512], F32, mix)
            TA = sb("TA", [P, EW], F32, mix)
            TB = sb("TB", [P, EW], F32, mix)
            wp = sb("wp", [P, 4, P], F32, mix)
            wg = sb("wg", [16, 2 * P], F32, mix)
            halo = sb("halo", [P, 4, HALO], F32, mix)
            vtmp = sb("vtmp", [P, CMAX], F32, mix)
            bl = sb("bl", [P, 2, 12], F32, mix)
            dec = sb("dec", [P, 2, 12], F32, mix)
        glr = vtmp
        kx = t1[0:NS, :, :].rearrange("p j n -> p (j n)")

        ps = [es.enter_context(nc.psum_tensor(f"bank{b}", [P, 512], F32)) for b in range(8)]

        s_x = sem("x_loaded"); s_small = sem("small_loaded"); s_ones = sem("ones_set")
        s_tr = sem("pe_start_transposes"); s_trev = sem("start_transposes_copied")
        s_cs = sem("silu_c_ready")
        s_aw = [sem(f"ada_weights_loaded{k}") for k in range(2)]
        s_apc = sem("ada_piece_used"); s_asel = sem("ada_selected"); s_aevc = sem("ada_sums_copied")
        s_ada = sem("ada_unit_stored"); s_coef = sem("norm_coefficients")
        s_ws = [sem(f"weight_loaded{k}") for k in range(NWS)]
        s_whi = sem("weight_high"); s_wsp = sem("weight_split")
        s_up = [sem("up_done1"), sem("up_done2")]; s_down = [sem("down_done1"), sem("down_done2")]
        s_silu = [sem("silu1"), sem("silu2")]; s_a = [sem("act_product1"), sem("act_product2")]
        s_ahi = [sem("act_high1"), sem("act_high2")]; s_act = [sem("act_split1"), sem("act_split2")]
        s_xacc = [sem("residual1"), sem("residual2")]
        n_sq = sem("norm_square"); n_add = sem("norm_added"); n_ss = sem("norm_sum")
        n_y = sem("norm_rsqrt"); n_v = sem("norm_rsqrt_refined"); n_yk = sem("norm_scaled"); n_hi = sem("norm_high"); n_lo = sem("norm_split")
        s_dve = sem("dve_step"); s_acts = sem("act_step"); s_pool = sem("pool_step")
        m_ld = sem("mix_inputs_loaded"); m_unit = sem("mix_unit_done"); m_ev = sem("proj_copied")
        m_gk = sem("gate_logits"); m_gkr = sem("gate_logits_read")
        m_pa = sem("prep_by_act"); m_pd = sem("prep_by_dve")
        m_vt = sem("v_turned"); m_vc = sem("v_copied")
        m_buf = sem("pool_buffers_turned"); m_bufc = sem("pool_buffers_copied")
        m_win = sem("window_sum"); m_p = sem("pooled"); m_z = sem("z_product"); m_zh = sem("z_high"); m_zs = sem("z_split")
        m_ut = sem("u_turned"); m_uc = sem("u_rows_copied"); m_ust = sem("u_rows_stored")
        m_init = sem("mix_zeroed")
        g_kt = sem("keys_turned"); g_kd = sem("keys_copied"); g_at = sem("scores"); g_am = sem("scores_masked")
        g_u = sem("state_update"); g_s = sem("state_ready"); g_o = sem("gla_out"); g_sq = sem("gla_square")
        g_ss = sem("gla_sum"); g_y = sem("gla_rsqrt"); g_w = sem("gla_scaled"); g_f = sem("gla_gated"); g_hi = sem("gla_high"); g_lo = sem("gla_split")
        g_kx = sem("masked_keys"); g_su = sem("sample_update"); g_s0 = sem("sample_state")
        m_x = sem("mix_residual"); m_st = sem("states_stored")
        s_ft = sem("final_turned"); s_fsq = sem("final_squares"); s_fl = sem("final_mean"); s_fy = sem("final_rsqrt"); s_fo = sem("final_scaled")
        s_out = [sem("y_stored0"), sem("y_stored1")]; s_lnf = sem("ln_final_loaded"); s_cp = sem("pool_rows_passed")

        block = es.enter_context(nc.Block())
        ident = cst[:, C_ID:C_ID + P]

        def sample_rows(g):
            return E[:, g, SB:SB + NSEQ * SW].rearrange("p (s w) -> p s w", w=SW)

        def sample_u(g):
            return sample_rows(g)[:, :, HALO:SW]

        def seqs(ap):
            return ap.rearrange("p (s t) -> p s t", t=TSEQ)

        def norm_bank(q):
            return ps[7] if 3 <= q < 6 else ps[4]

        def cols(w, c0):
            return w[:, c0:c0 + P].rearrange("(k p) n -> p k n", p=P)

        @block.sync
        def _(sp):
            sp.dma_start(cst[:, :], i["const"]).then_inc(s_small, 16)
            sp.dma_start(cin[0:1, :], i["c_prompt"]).then_inc(s_small, 16)
            sp.dma_start(cin[1:9, :], i["c_sample"]).then_inc(s_small, 16)
            for name, r, n in (("b_ada", R_BADA, 72), ("ln_ffn1", R_LN1, 8), ("ln_mix", R_LNM, 8), ("ln_ffn2", R_LN2, 8),
                               ("b_gk2", R_BGK, 2), ("pool_scale", R_PS, 4), ("gla_norm", R_GN, 1)):
                sp.dma_start(vin[r:r + n, :], i[name].rearrange("a (r p) -> (a r) p", p=P)).then_inc(s_small, 16)
            for t in range(8):
                sp.dma_start(xin[:, t, :], i["x_prompt"][0, P * t:P * (t + 1), :]).then_inc(s_x, 16)
            sp.dma_start(xin[0:NS, 8, :], i["x_sample"].rearrange("b t d -> (b t) d")).then_inc(s_x, 16)
            sp.dma_start(o["pool_s"][0, :, 0:HALO - TSEQ, :], i["state_pool"][0, :, TSEQ:HALO, :]).then_inc(s_cp, 16)

            def load_w(n, slot, src, trip=0):
                if not isinstance(n, int) or n >= NWS:
                    sp.wait_ge(s_wsp, n - NWS + 1)
                sp.dma_start(ws[:, slot, :].rearrange("p (k n) -> p k n", n=P) if len(src.shape) == 3 else ws[:, slot, :],
                             src).then_inc(s_ws[slot], 16)

            def load_ada(n, slot, src):
                if not isinstance(n, int) or n >= 2:
                    sp.wait_ge(s_apc, n - 1)
                sp.dma_start(aws[:, slot, :], src).then_inc(s_aw[slot], 16)

            def ffn_tiles(up, down, base, b, adas=None):
                srcs = []
                for f in range(FB):
                    for half in range(2):
                        c0 = b * (FB * P) + (F * half + P * f)
                        srcs.append(up[:, bass.ds(c0, P)].rearrange("(k p) n -> p k n", p=P))
                for f in range(FB):
                    srcs.append(down[bass.ds(b * (FB * P) + P * f, P), :])
                for t, src in enumerate(srcs):
                    load_w(b * 6 + (base + t), (base + t) % NWS, src)
                if adas is not None:
                    for k in range(KT):
                        load_ada(b * KT + (AU_FIRST * KT + k), k % 2,
                                 i["w_ada"][P * k:P * (k + 1), bass.ds(b * AU + AU_FIRST * AU, AU)])

            for u in range(AU_FIRST):
                for k in range(KT):
                    load_ada(u * KT + k, k % 2, i["w_ada"][P * k:P * (k + 1), AU * u:AU * (u + 1)])
            ffn_tiles(i["w_ffn1_up"], i["w_ffn1_down"], W_F1, 0, True)
            with sp.Fori(1, NB) as b:
                ffn_tiles(i["w_ffn1_up"], i["w_ffn1_down"], W_F1, b, True)
            for c in range(NC):
                for u in range(UPC):
                    n = W_MIX + UPC * c + u
                    src = cols(i["w_in"], PROJ[u][2]) if u < NPROJ else cols(i["w_out"], P * (u - NPROJ))
                    load_w(n, n % NWS, src)
                    if c == 0 and u == 0:
                        sp.wait_ge(s_down[0], 24 * NB)
                        sp.wait_ge(s_act[0], 6 * NB)
                        sp.dma_start(wg[:, :], i["w_gk2"]).then_inc(m_ld, 16)
                        sp.dma_start(wp[:, :, :], i["w_pool"].rearrange("g p n -> p g n")).then_inc(m_ld, 16)
                        sp.dma_start(rows[0:NSEQ * HALO, :], i["state_pool"].rearrange("a b r d -> (a b r) d")).then_inc(m_ld, 16)
                        for j in range(2):
                            sp.dma_start(S0[:, j, :, :], i["state_gla"][0, :, 2 * j:2 * j + 2, :, :]
                                         .rearrange("s h d e -> (h d) s e")).then_inc(m_ld, 16)
                    if c == 2 and u == UPC - 1:
                        sp.wait_ge(m_uc, 1)
                        sp.dma_start(o["pool_p"][0, 0, :, :], rows[0:HALO, :]).then_inc(m_ust, 16)
                        sp.wait_ge(m_uc, 2)
                        sp.dma_start(o["pool_s"][0, :, HALO - TSEQ:HALO, :], rows[NS:2 * NS, :]).then_inc(m_ust, 16)
                        sp.wait_ge(g_s, 16)
                        for j in range(2):
                            sp.dma_start(o["gla_p"][0, 0, 2 * j:2 * j + 2, :, :].rearrange("h d e -> (h d) e"),
                                         S[:, 16 % 3, j, :]).then_inc(m_st, 16)
                        sp.wait_ge(g_s0, NSEQ)
                        for j in range(2):
                            sp.dma_start(o["gla_s"][0, :, 2 * j:2 * j + 2, :, :].rearrange("s h d e -> (h d) s e"),
                                         S0[:, j, :, :]).then_inc(m_st, 16)
            sp.wait_ge(s_down[0], 24 * NB)
            ffn_tiles(i["w_ffn2_up"], i["w_ffn2_down"], W_F2, 0)
            with sp.Fori(1, NB) as b:
                ffn_tiles(i["w_ffn2_up"], i["w_ffn2_down"], W_F2, b)
            sp.dma_start(lnf[:, :], i["ln_final"].rearrange("(a d) -> a d", a=1).broadcast_to([P, D])).then_inc(s_lnf, 16)
            yp = o["y_p"][0].rearrange("(t p) d -> t p d", p=P)
            for t in range(9):
                sp.wait_ge(s_fo, t + 1)
                if t < 8:
                    sp.dma_start(yp[t], yst[:, t % 2, :]).then_inc(s_out[t % 2], 16)
                else:
                    sp.dma_start(o["y_s"].rearrange("b t d -> (b t) d"), yst[0:NS, t % 2, :]).then_inc(s_out[t % 2], 16)
            sp.wait_ge(s_out[0], 16 * 5)
            sp.wait_ge(s_out[1], 16 * 4)
            sp.wait_ge(m_ust, 32)
            sp.wait_ge(m_st, 64)
            sp.wait_ge(s_cp, 16)

        @block.tensor
        def _(pe):
            def split_product(out, w_hi, w_lo, x_hi, x_lo, depth):
                for k in range(depth):
                    for a, (l, r) in enumerate(((w_hi, x_hi), (w_hi, x_lo), (w_lo, x_hi))):
                        mm = pe.matmul(out, l(k), r(k), start=(k == 0 and a == 0), stop=(k == depth - 1 and a == 2))
                return mm

            def ada_piece(n, k, slot):
                pe.wait_ge(s_aw[slot], n * 64 + 16 * (k // 2 + 1))
                q = k % 4
                pe.matmul(ps[7][32 * q:32 * q + 32, :], csT[:, k, :], aws[:, slot, :],
                          start=(k < 4), stop=(k >= 4)).then_inc(s_apc, 1)

            def ada_select():
                for a in range(4):
                    mm = pe.matmul(ps[7][:, 10 * a:10 * a + 10], aev[:, P * a:P * (a + 1)], cst[:, C_SEL:C_SEL + 10],
                                   start=True, stop=True)
                mm.then_inc(s_asel, 1)

            def ones_sum(q, n):
                pe.wait_ge(n_add, KT * (q + 1))
                if q:
                    pe.wait_ge(n_v, q)
                pe.matmul(norm_bank(q)[:, 0:n], ones[:, :], tb(2)[:, 0:n], start=True, stop=True).then_inc(n_ss, 1)

            def ffn(which, base, b, q0, adas, first):
                whi = lambda s: (lambda k: wh[:, s, P * k:P * (k + 1)])
                wlo = lambda s: (lambda k: wl[:, s, P * k:P * (k + 1)])
                for u in range(3 * FB):
                    f, c = divmod(u, 3)
                    sl = slice(CH0[c], CH0[c] + CHN[c])
                    if first and f == 0:
                        if c > 0:
                            ones_sum(q0 + c, CHN[c])
                        pe.wait_ge(n_lo, KT * (q0 + c + 1))
                    if c == 0:
                        pe.wait_ge(s_wsp, b * 6 + (base + 2 * f + 2))
                    if not (first and u < 2):
                        pe.wait_ge(s_a[which], b * 6 + (u - 1))
                    for half in range(2):
                        bank = ps[2 * (u % 2) + half][:, 0:CHN[c]]
                        s = 2 * f + half
                        mm = split_product(bank, whi(s), wlo(s), lambda k: hh[:, k, sl], lambda k: hl[:, k, sl], KT)
                    mm.then_inc(s_up[which], 1)
                    if adas:
                        if u < 4:
                            if u == 0:
                                pe.wait_ge(s_ada, b + AU_FIRST)
                            ada_piece(b + AU_FIRST, 2 * u, 0)
                            ada_piece(b + AU_FIRST, 2 * u + 1, 1)
                pe.wait_ge(s_wsp, b * 6 + (base + 6))
                for c in range(NC):
                    sl = slice(CH0[c], CH0[c] + CHN[c])
                    pe.wait_ge(s_act[which], b * 6 + (4 + c))
                    for m in range(KT):
                        n = KT * c + m
                        if not (first and n < 3):
                            pe.wait_ge(s_xacc[which], b * 24 + (n - 2))
                        split_product(ps[4 + n % 3][:, 0:CHN[c]], lambda k: wh[:, 4 + k, P * m:P * (m + 1)],
                                      lambda k: wl[:, 4 + k, P * m:P * (m + 1)], lambda k: ah[:, k, sl],
                                      lambda k: al[:, k, sl], FB).then_inc(s_down[which], 1)
                    if adas and c == 0:
                        pe.wait_ge(s_aevc, b + (AU_FIRST + 1))
                        ada_select()

            pe.wait_ge(s_small, 16 * 10)
            pe.transpose(ps[0][:, 0:R_END], vin[:, :], cst[0:R_END, C_ID:C_ID + R_END]).then_inc(s_tr, 1)
            for k in range(KT):
                mm = pe.transpose(ps[1][:, 9 * k:9 * k + 9], cin[:, P * k:P * (k + 1)], cst[0:9, C_ID:C_ID + 9])
            mm.then_inc(s_tr, 1)
            pe.wait_ge(s_x, 16 * 9)
            for t in range(9):
                n = P if t < 8 else NS
                for a in range(2):
                    bank = 2 + (2 * t + a) % 4
                    if 2 * t + a >= 4:
                        pe.wait_ge(s_trev, 2 * t + a - 3)
                    for k in range(4):
                        mm = pe.transpose(ps[bank][:, n * k:n * k + n], xin[0:n, t, P * (4 * a + k):P * (4 * a + k + 1)],
                                          cst[0:n, C_ID:C_ID + n])
                    mm.then_inc(s_tr, 1)
            pe.wait_ge(s_cs, 2)
            for u in range(AU_FIRST):
                if u:
                    pe.wait_ge(s_ada, u)
                for k in range(KT):
                    ada_piece(u, k, k % 2)
                pe.wait_ge(s_aevc, u + 1)
                ada_select()
            pe.wait_ge(s_ada, AU_FIRST)
            pe.wait_ge(s_ones, 1)
            pe.wait_ge(s_trev, 18)
            ones_sum(0, CHN[0])
            ffn(0, W_F1, 0, 0, True, True)
            with pe.Fori(1, NB) as b:
                ffn(0, W_F1, b, 0, True, False)

            pe.wait_ge(s_ada, NAU)
            pe.wait_ge(s_xacc[0], 24 * NB)
            pe.wait_ge(m_ld, 16 * 5)
            for c in range(NC):
                n = CHN[c]
                sl = slice(CH0[c], CH0[c] + n)
                tiles = PAIRS[c] + (c == 2)

                def unit(u):
                    g = UPC * c + u
                    pe.wait_ge(s_wsp, W_MIX + g + 1)
                    s = g % 2
                    split_product(ps[u % RING][:, 0:n] if u < NPROJ else ps[(u - NPROJ) % RING][:, 0:n],
                                  lambda k: mwh[:, s, P * k:P * (k + 1)], lambda k: mwl[:, s, P * k:P * (k + 1)],
                                  lambda k: hh[:, k, sl], lambda k: hl[:, k, sl], KT).then_inc(m_unit, 1)

                def turn_v(h):
                    pe.wait_ge(m_ev, NPROJ * c + IDX["v", h] + 1)
                    v = 4 * c + h
                    if h >= 2 or c:
                        pe.wait_ge(m_vc, v - 1)
                    if h < 2:
                        pe.wait_ge(m_gkr, 2 * (c + 1))
                    for t in range(tiles):
                        w = NS if c == 2 and t == 2 else P
                        mm = pe.transpose(ps[6 + h % 2][0:w, P * t:P * (t + 1)], vtmp[:, P * t:P * t + w], ident)
                    mm.then_inc(m_vt, 1)

                if c == 0:
                    ones_sum(3, n)
                pe.wait_ge(n_lo, KT * (3 + c + 1))
                if c == 2:
                    for g in range(4):
                        mm = pe.transpose(ps[6][:, 120 * g:120 * (g + 1)], rows[0:120, P * g:P * (g + 1)],
                                          cst[0:120, C_ID:C_ID + 120])
                    mm.then_inc(m_buf, 1)
                for u in range(NPROJ):
                    if u >= RING:
                        pe.wait_ge(m_ev, NPROJ * c + u - RING + 1)
                    elif c:
                        pe.wait_ge(m_x, KT * c)
                    unit(u)
                    if c == 0 and u < 2:
                        ones_sum(4 + u, CHN[1 + u])
                    if u == 3:
                        pe.wait_ge(m_ev, NPROJ * c + 1)
                        if c == 0:
                            pe.wait_ge(n_v, 6)
                        if c == 2:
                            pe.wait_ge(m_bufc, 1)
                        for j in range(2):
                            pe.matmul(ps[6 + j][:, 0:n], wg[:, P * j:P * (j + 1)], glr[0:16, 0:n],
                                      start=True, stop=True).then_inc(m_gk, 1)
                    if 6 <= u < 10:
                        turn_v(u - 6)
                    if c == 2 and u == 13:
                        pe.wait_ge(m_ev, NPROJ * c + IDX["u", 3] + 1)
                        pe.wait_ge(m_vc, 4 * (c + 1))
                        for g in range(4):
                            mm = pe.transpose(ps[6][0:HALO, P * g:P * (g + 1)], E[:, g, LASTP:LASTP + HALO], ident)
                        mm.then_inc(m_ut, 1)
                        for g in range(4):
                            mm = pe.transpose(ps[7][0:NS, P * g:P * (g + 1)], vtmp[:, NS * g:NS * (g + 1)], ident)
                        mm.then_inc(m_ut, 1)
                pe.wait_ge(m_ev, NPROJ * (c + 1))
                pe.wait_ge(m_vc, 4 * (c + 1))
                for g in range(4):
                    pe.wait_ge(m_p, 4 * c + g + 1)
                    np_ = n if c < 2 else LASTP
                    mm = pe.matmul(ps[g][:, 0:np_], wp[:, g, :], E[:, g, HALO:HALO + np_], start=True, stop=True)
                    if c == 2:
                        mm = pe.matmul(ps[g][:, np_:n], wp[:, g, :],
                                       sample_u(g),
                                       start=True, stop=True)
                    mm.then_inc(m_z, 1)
                pe.wait_ge(m_pd, 4 * (c + 1))
                pe.wait_ge(m_zs, 4 * (c + 1))
                if c == 2:
                    pe.wait_ge(m_uc, 2)
                for p in range(tiles):
                    t = 3 * c + p
                    w = NS if t == 8 else P
                    cs = slice(P * p, P * p + w)
                    if t:
                        pe.wait_ge(g_kd, t)
                    for j in range(2):
                        mm = pe.transpose(ps[6][0:w, P * j:P * (j + 1)], bs[:, j, cs], ident)
                    mm.then_inc(g_kt, 1)
                    if t:
                        pe.wait_ge(g_am, t)
                    for h in range(HEADS):
                        r = slice(DK * (h % 2), DK * (h % 2) + DK)
                        for a in range(w // GC):
                            cc = slice(P * p + GC * a, P * p + GC * (a + 1))
                            mm = pe.matmul(ps[h % 2][GC * a:GC * (a + 1), GC * (h // 2):GC * (h // 2 + 1)],
                                           ks[r, h // 2, cc], qs[r, h // 2, cc], start=True, stop=True)
                    mm.then_inc(g_at, 1)
                    pe.wait_ge(g_kd, t + 1)
                    if t < 8:
                        for a in range(2):
                            if 2 * t + a >= 2:
                                pe.wait_ge(g_s, 2 * t + a - 1)
                            for h in range(HEADS):
                                mm = pe.matmul(ps[4 + a][DK * (h % 2):DK * (h % 2) + DK, P * (h // 2):P * (h // 2 + 1)],
                                               kdT[GC * a:GC * (a + 1), DK * h:DK * (h + 1)],
                                               vs[GC * a:GC * (a + 1), p, DV * h:DV * (h + 1)], start=True, stop=True)
                            mm.then_inc(g_u, 1)
                    pe.wait_ge(g_am, t + 1)
                    if t:
                        pe.wait_ge(g_w, t)
                    if t < 8:
                        pe.wait_ge(g_s, 2 * t + 1)
                    if t == 0:
                        pe.wait_ge(m_init, 2)
                    for h in range(HEADS):
                        r = slice(DK * (h % 2), DK * (h % 2) + DK)
                        ob = ps[2 + h % 2][:, P * (h // 2):P * (h // 2) + w]
                        pe.matmul(ob, vs[:, p, DV * h:DV * (h + 1)], attS[:, h, 0:w], start=True, stop=False)
                        if t < 8:
                            for a in range(2):
                                mm = pe.matmul(ob[:, GC * a:GC * (a + 1)], S[r, (2 * t + a) % 3, h // 2, :],
                                               qs[r, h // 2, P * p + GC * a:P * p + GC * (a + 1)], start=False, stop=(a == 1))
                        else:
                            for s in range(NSEQ):
                                mm = pe.matmul(ob[:, TSEQ * s:TSEQ * (s + 1)], S0[r, h // 2, s, :],
                                               qs[r, h // 2, P * p + TSEQ * s:P * p + TSEQ * (s + 1)], start=False, stop=(s == NSEQ - 1))
                    mm.then_inc(g_o, 1)
                    pe.wait_ge(g_sq, t + 1)
                    if t:
                        pe.wait_ge(g_w, t)
                    pe.matmul(ps[7][:, 0:4 * w], ones[:, :], tmp[:, 0:4 * w], start=True, stop=True).then_inc(g_ss, 1)
                    if t == 8:
                        for s in range(NSEQ):
                            pe.wait_ge(g_kx, s + 1)
                            if s >= 2:
                                pe.wait_ge(g_s0, s - 1)
                            else:
                                pe.wait_ge(g_s, 16)
                            for h in range(HEADS):
                                mm = pe.matmul(ps[4 + s % 2][DK * (h % 2):DK * (h % 2) + DK, P * (h // 2):P * (h // 2 + 1)],
                                               kx[:, 256 * (s % 2) + DK * h:256 * (s % 2) + DK * (h + 1)],
                                               vs[0:NS, p, DV * h:DV * (h + 1)], start=True, stop=True)
                            mm.then_inc(g_su, 1)
                done = 3 * c + tiles
                pe.wait_ge(g_lo, 2 * done)
                pe.wait_ge(g_s, 2 * min(done, 8))
                if c == 2:
                    pe.wait_ge(g_s0, NSEQ)
                for m in range(KT):
                    if m >= RING:
                        pe.wait_ge(m_x, KT * c + m - RING + 1)
                    unit(NPROJ + m)
            pe.wait_ge(m_x, KT * NC)
            ones_sum(6, CHN[0])
            ffn(1, W_F2, 0, 6, False, True)
            with pe.Fori(1, NB) as b:
                ffn(1, W_F2, b, 6, False, False)
            pe.wait_ge(s_xacc[1], 24 * NB)
            for t in range(9):
                w = P if t < 8 else NS
                if t >= 2:
                    pe.wait_ge(s_fo, t - 1)
                for k in range(KT):
                    mm = pe.transpose(ps[2 * (t % 2) + k // 4][0:w, P * (k % 4):P * (k % 4 + 1)], xT[:, k, P * t:P * t + w], ident)
                mm.then_inc(s_ft, 1)

        @block.scalar
        def _(act):
            step = Steps(act, s_acts)

            def split_hi(n, slot, dst):
                if isinstance(n, int):
                    act.wait_ge(s_ws[slot], 16 * (n // NWS + 1))
                else:
                    act.wait_ge(s_ws[slot], n[0] * 32 + 16 * (n[1] // NWS + 1))
                act.activation(dst, ws[:, slot, :], ACT.Copy).then_inc(s_whi, 1)

            def norm(q, c):
                n = CHN[c]
                for k in range(KT):
                    if k >= 2:
                        act.wait_ge(n_add, KT * q + k - 1)
                    elif q:
                        act.wait_ge(n_lo, KT * q)
                    act.activation(tb(k % 2)[:, 0:n], xT[:, k, CH0[c]:CH0[c] + n], ACT.Square).then_inc(n_sq, 1)
                act.wait_ge(n_ss, q + 1)
                step(act.activation(tb(0)[:, 0:n], norm_bank(q)[:, 0:n], ACT.Ln, scale=1.0 / D, bias=EPS))
                act.activation(tb(1)[:, 0:n], tb(0)[:, 0:n], ACT.Exp, scale=-0.5).then_inc(n_y, 1)
                sh = ada[:, (0, 3 * KT, 6 * KT)[q // 3]:(KT, 4 * KT, 7 * KT)[q // 3], :]
                m = n if c < 2 else LASTP
                for k in range(KT):
                    act.wait_ge(n_yk, KT * q + k + 1)
                    ins = act.activation(hh[:, k, CH0[c]:CH0[c] + m], tb(3 + k % 2)[:, 0:m], ACT.Identity, bias=sh[:, k, 0:1])
                    if c == 2:
                        ins = act.activation(hh[:, k, SEQ:TOK], tb(3 + k % 2)[:, m:n], ACT.Copy)
                    ins.then_inc(n_hi, 1)

            def ffn(which, base, b, first, last):
                for u in range(3 * FB):
                    f, c = divmod(u, 3)
                    n = CHN[c]
                    act.wait_ge(s_up[which], b * 6 + (u + 1))
                    if not (first and u == 0):
                        act.wait_ge(s_a[which], b * 6 + u)
                    act.activation(tb(6)[:, 0:n], ps[2 * (u % 2)][:, 0:n], ACT.Silu).then_inc(s_silu[which], 1)
                    if not (first and u == 0):
                        pass
                    act.wait_ge(s_a[which], b * 6 + (u + 1))
                    act.activation(ah[:, f, CH0[c]:CH0[c] + n], tb(7)[:, 0:n], ACT.Copy).then_inc(s_ahi[which], 1)
                    if u == 0:
                        if not first:
                            act.wait_ge(s_down[which], b * 24)
                        for t in (4, 5):
                            split_hi((b * 1, base + t) if not isinstance(b, int) else b * 6 + base + t, t % 3, wh[:, t, :])
                    if u == 3 and not last:
                        for t in (0, 1):
                            split_hi((b, base + 6 + t) if not isinstance(b, int) else b * 6 + base + 6 + t, t % 3, wh[:, t, :])
                if not last:
                    for t in (2, 3):
                        split_hi((b, base + 6 + t) if not isinstance(b, int) else b * 6 + base + 6 + t, t % 3, wh[:, t, :])

            act.wait_ge(s_tr, 2)
            act.wait_ge(s_cs, 1)
            act.activation(csT[:, :, 0:9], ps[1][:, 0:9 * KT].rearrange("p (k s) -> p k s", s=9), ACT.Silu).then_inc(s_cs, 1)
            act.wait_ge(s_trev, 18)
            norm(0, 0)
            act.wait_ge(s_tr, 20)
            for t in range(4):
                split_hi(t, t % NWS, wh[:, t, :])
            norm(1, 1)
            norm(2, 2)
            ffn(0, W_F1, 0, True, False)
            with act.Fori(1, NB - 1) as b:
                ffn(0, W_F1, b, False, False)
            ffn(0, W_F1, NB - 1, False, True)

            act.wait_ge(s_down[0], 24 * NB)
            for g in range(2):
                split_hi(W_MIX + g, g % NWS, mwh[:, g, :])
            act.wait_ge(s_xacc[0], 24 * (NB - 1) + KT)
            norm(3, 0)

            for c in range(NC):
                n = CHN[c]
                tiles = PAIRS[c] + (c == 2)
                for u in range(UPC):
                    g = UPC * c + u
                    if u == NPROJ:
                        for p in range(tiles):
                            t = 3 * c + p
                            w = NS if t == 8 else P
                            act.wait_ge(g_o, t + 1)
                            for a in range(2):
                                ins = act.activation(tmp[:, 2 * w * a:2 * w * (a + 1)].rearrange("p (j n) -> p j n", j=2),
                                                     ps[2 + a][:, 0:2 * P].rearrange("p (j n) -> p j n", j=2)[:, :, 0:w], ACT.Square)
                            ins.then_inc(g_sq, 1)
                            act.wait_ge(g_ss, t + 1)
                            step(act.activation(tmp[:, 512:512 + 4 * w], ps[7][:, 0:4 * w], ACT.Ln, scale=1.0 / DV, bias=EPS))
                            act.activation(tmp[:, 1024:1024 + 4 * w], tmp[:, 512:512 + 4 * w], ACT.Exp, scale=-0.5).then_inc(g_y, 1)
                            act.wait_ge(g_f, t + 1)
                            for a in range(2):
                                ins = act.activation(hh[:, 4 + a:8:2, P * t:P * t + w],
                                                     tmp[:, 2048 + 2 * w * a:2048 + 2 * w * (a + 1)].rearrange("p (j n) -> p j n", j=2), ACT.Copy)
                            ins.then_inc(g_hi, 1)
                    act.wait_ge(m_unit, g + 1)
                    if g + 2 < UPC * NC:
                        split_hi(W_MIX + g + 2, (g + 2) % NWS, mwh[:, g % 2, :])
                    elif g + 2 == UPC * NC:
                        act.wait_ge(m_st, 64)
                        act.wait_ge(m_ust, 32)
                        act.wait_ge(g_s0, NSEQ)
                        for t in range(4):
                            split_hi(W_F2 + t, t % NWS, wh[:, t, :])
                    if u < NPROJ:
                        kind, j, _ = PROJ[u]
                        bank = ps[u % RING]
                        if kind == "glr":
                            if c:
                                act.wait_ge(m_vt, 4 * c)
                            act.activation(glr[0:16, 0:n], bank[0:16, 0:n], ACT.Copy).then_inc(m_ev, 1)
                        elif kind == "k":
                            act.activation(ks[:, j, 0:n], bank[:, 0:n], ACT.Copy).then_inc(m_ev, 1)
                        elif kind == "q":
                            act.activation(qs[:, j, 0:n], bank[:, 0:n], ACT.Copy).then_inc(m_ev, 1)
                        elif kind == "v":
                            if j == 0:
                                act.wait_ge(m_gk, 2 * (c + 1))
                            else:
                                act.wait_ge(m_vt, 4 * c + j)
                            act.activation(vtmp[:, 0:n], bank[:, 0:n], ACT.Copy).then_inc(m_ev, 1)
                        elif kind == "u":
                            m = n if c < 2 else LASTP
                            if c:
                                act.wait_ge(m_z, 4 * c)
                            ins = act.activation(E[:, j, HALO:HALO + m], bank[:, 0:m], ACT.Copy)
                            if c == 2:
                                act.activation(sample_u(j), seqs(bank[:, m:n]), ACT.Copy)
                                act.wait_ge(m_vt, 4 * (c + 1))
                                ins = act.activation(vtmp[:, NS * j:NS * (j + 1)], bank[:, m:n], ACT.Copy)
                            ins.then_inc(m_ev, 1)
                        else:
                            act.activation(og[:, j, 0:n], bank[:, 0:n], ACT.Silu).then_inc(m_ev, 1)
                    if c == 0 and u < 2:
                        act.wait_ge(s_xacc[0], 24 * (NB - 1) + KT * (u + 2))
                        norm(4 + u, 1 + u)
                    if u == 4:
                        act.wait_ge(m_gk, 2 * (c + 1))
                        for j in range(2):
                            ins = act.activation(t1[:, j, 0:n], ps[6 + j][:, 0:n], ACT.Abs, bias=vec[:, R_BGK + j:R_BGK + j + 1])
                        step(ins)
                        step(act.activation(t1[:, :, 0:n], t1[:, :, 0:n], ACT.Exp, scale=-1.0))
                        act.activation(t1[:, :, 0:n], t1[:, :, 0:n], ACT.Ln, bias=1.0).then_inc(m_pa, 1)
                    if u == 5:
                        act.wait_ge(m_pd, 4 * c + 1)
                        act.activation(t1[:, :, 0:n], bs[:, :, 0:n], ACT.Exp, scale=1.0 / 16).then_inc(m_pa, 1)
                    if u == 6:
                        act.wait_ge(m_pd, 4 * c + 2)
                        act.activation(t1[:, :, 0:n], bs[:, :, 0:n], ACT.Exp, scale=-1.0 / 16)
                        act.activation(dec[:, :, :], bl[:, :, :], ACT.Exp, scale=1.0 / 16).then_inc(m_pa, 1)
                    if u == 7:
                        act.wait_ge(m_pd, 4 * c + 3)
                        act.activation(bs[:, :, 0:n], bs[:, :, 0:n], ACT.Exp, scale=1.0 / 16).then_inc(m_pa, 1)
                    if u == NPROJ - 1:
                        for gg in range(4):
                            m = n
                            act.wait_ge(m_z, 4 * c + gg + 1)
                            act.activation(hh[:, gg, CH0[c]:CH0[c] + n], ps[gg][:, 0:n], ACT.Copy, scale=vec[:, R_PS + gg:R_PS + gg + 1]).then_inc(m_zh, 1)
            for q in range(6, 9):
                act.wait_ge(m_x, KT * NC)
                norm(q, q - 6)
            ffn(1, W_F2, 0, True, False)
            with act.Fori(1, NB - 1) as b:
                ffn(1, W_F2, b, False, False)
            ffn(1, W_F2, NB - 1, False, True)
            for t in range(9):
                w = P if t < 8 else NS
                act.wait_ge(s_ft, t + 1)
                for a in range(2):
                    step(act.activation(tmp[0:w, 0:512], ps[2 * (t % 2) + a][0:w, :], ACT.Square, accum_out=rsf[0:w, t, a:a + 1]))
                step(act.activation(rsf[0:w, t, 2:3], rsf[0:w, t, 0:1], ACT.Identity, bias=rsf[0:w, t, 1:2]))
                step(act.activation(rsf[0:w, t, 3:4], rsf[0:w, t, 2:3], ACT.Ln, scale=1.0 / D, bias=EPS))
                act.activation(rsf[0:w, t, 4:5], rsf[0:w, t, 3:4], ACT.Exp, scale=-0.5).then_inc(s_fy, 1)

        @block.gpsimd
        def _(gp):
            gp.memset(csT[:, :, :], 0.0).then_inc(s_cs, 1)
            gp.memset(ones[:, :], 1.0).then_inc(s_ones, 1)

            def norm(q, c):
                n = CHN[c]
                if q:
                    gp.wait_ge(n_ss, q)
                for k in range(KT):
                    gp.wait_ge(n_sq, KT * q + k + 1)
                    if k == 0:
                        gp.tensor_copy(tb(2)[:, 0:n], tb(0)[:, 0:n]).then_inc(n_add, 1)
                    else:
                        gp.wait_ge(n_add, KT * q + k)
                        gp.tensor_tensor(tb(2)[:, 0:n], tb(2)[:, 0:n], tb(k % 2)[:, 0:n], ALU.add).then_inc(n_add, 1)

            for q in range(6):
                norm(q, q % 3)
            gp.wait_ge(s_down[0], 24 * NB)
            gp.wait_ge(s_act[0], 6 * NB)
            gp.wait_ge(m_unit, 1)
            gp.memset(attS[:, :, :], 0.0).then_inc(m_init, 1)
            gp.memset(S[:, 0, :, :], 0.0).then_inc(m_init, 1)
            step = Steps(gp, s_pool)
            step(gp.memset(halo[:, :, :], 0.0))
            for c in range(NC):
                m = CHN[c] if c < 2 else LASTP
                W = HALO + m if c < 2 else EW
                if c == 2:
                    gp.wait_ge(m_bufc, 1)
                for g in range(4):
                    gp.wait_ge(m_ev, NPROJ * c + IDX["u", g] + 1)
                    step(gp.tensor_copy(E[:, g, 0:HALO], halo[:, g, :]))
                    if c < 2:
                        step(gp.tensor_copy(halo[:, g, :], E[:, g, m:m + HALO]))
                    if g or c:
                        gp.wait_ge(m_p, 4 * c + g)
                    lo = 0
                    for k in range(g + 1):
                        dst = (TA, TB)[k % 2]
                        src = E[:, g, :] if k == 0 else (TB, TA)[k % 2][:, :]
                        lo += 1 << k
                        ins = gp.tensor_tensor(dst[:, lo:W], src[:, lo:W], src[:, lo - (1 << k):W - (1 << k)], ALU.add)
                        if k < g or c == 0:
                            step(ins)
                    if c == 0:
                        ins = gp.tensor_tensor(dst[:, HALO:2 * HALO], dst[:, HALO:2 * HALO],
                                               cst[:, C_RATIO + HALO * g:C_RATIO + HALO * (g + 1)], ALU.mult)
                    ins.then_inc(m_win, 1)
            for q in range(6, 9):
                norm(q, q - 6)

        @block.vector
        def _(dve):
            step = Steps(dve, s_dve)

            def split_lo(n, slot, dst, high):
                dve.wait_ge(s_whi, n + 1)
                dve.tensor_tensor(dst, ws[:, slot, :], high.bitcast(F32), ALU.subtract).then_inc(s_wsp, 1)

            def norm(q, c):
                n = CHN[c]
                m = n if c < 2 else LASTP
                sl = slice(CH0[c], CH0[c] + n)
                k0 = (0, 3 * KT, 6 * KT)[q // 3]
                sh, co = ada[:, k0:k0 + KT, :], coef[:, q // 3, :, :]
                v, t3, R = tb(3)[:, 0:n], tb(4)[:, 0:n], tb(5)[:, 0:n]
                dve.wait_ge(n_y, q + 1)
                if q:
                    dve.wait_ge(n_lo, KT * q)
                y = tb(1)[:, 0:n]
                dve.tensor_scalar(v, norm_bank(q)[:, 0:n], 1.0 / D, EPS, ALU.mult, ALU.add)
                step(dve.tensor_tensor(t3, y, y, ALU.mult))
                step(dve.scalar_tensor_tensor(out=t3, in0=t3, scalar=-0.5, in1=v, op0=ALU.mult, op1=ALU.mult))
                dve.scalar_tensor_tensor(out=R, in0=t3, scalar=1.5, in1=y, op0=ALU.add, op1=ALU.mult).then_inc(n_v, 1)
                dve.wait_ge(n_v, q + 1)

                def scaled(k):
                    yb = tb(3 + k % 2)
                    ins = dve.scalar_tensor_tensor(out=yb[:, 0:m], in0=xT[:, k, CH0[c]:CH0[c] + m], scalar=co[:, k, 0:1],
                                                   in1=R[:, 0:m], op0=ALU.mult, op1=ALU.mult)
                    if c == 2:
                        step(dve.tensor_tensor(yb[:, m:n], xT[:, k, SEQ:TOK], R[:, m:n], ALU.mult))
                        step(dve.tensor_tensor(seqs(yb[:, m:n]), seqs(yb[:, m:n]),
                                               co[:, k, 1:9].unsqueeze(2).broadcast_to([P, NSEQ, TSEQ]), ALU.mult))
                        ins = dve.tensor_tensor(seqs(yb[:, m:n]), seqs(yb[:, m:n]),
                                                sh[:, k, 1:9].unsqueeze(2).broadcast_to([P, NSEQ, TSEQ]), ALU.add)
                    ins.then_inc(n_yk, 1)

                scaled(0)
                for k in range(KT):
                    if k + 1 < KT:
                        if k:
                            dve.wait_ge(n_lo, KT * q + k)
                        scaled(k + 1)
                    yb = tb(3 + k % 2)
                    dve.wait_ge(n_hi, KT * q + k + 1)
                    ins = dve.scalar_tensor_tensor(out=hl[:, k, CH0[c]:CH0[c] + m], in0=yb[:, 0:m], scalar=sh[:, k, 0:1],
                                                   in1=hh[:, k, CH0[c]:CH0[c] + m].bitcast(F32), op0=ALU.add, op1=ALU.subtract)
                    if c == 2:
                        ins = dve.tensor_tensor(hl[:, k, SEQ:TOK], yb[:, m:n], hh[:, k, SEQ:TOK].bitcast(F32), ALU.subtract)
                    ins.then_inc(n_lo, 1)

            def add_residual(bank, k, c, gain, done):
                m = CHN[c] if c < 2 else LASTP
                xs = xT[:, k, CH0[c]:CH0[c] + m]
                ins = dve.scalar_tensor_tensor(out=xs, in0=bank[:, 0:m], scalar=ada[:, gain + k, 0:1], in1=xs, op0=ALU.mult, op1=ALU.add)
                if c == 2:
                    t = tb(5)[:, NS * (k % 2):NS * (k % 2 + 1)]
                    step(dve.tensor_tensor(seqs(t), seqs(bank[:, m:m + NS]),
                                           ada[:, gain + k, 1:9].unsqueeze(2).broadcast_to([P, NSEQ, TSEQ]), ALU.mult))
                    ins = dve.tensor_tensor(xT[:, k, SEQ:TOK], xT[:, k, SEQ:TOK], t, ALU.add)
                ins.then_inc(done, 1)

            def ada_sums(n):
                dve.wait_ge(s_apc, n * KT + KT)
                dve.tensor_copy(aev[:, :], ps[7][:, :]).then_inc(s_aevc, 1)

            def ada_store(n):
                dve.wait_ge(s_asel, n + 1)
                dve.tensor_tensor(ada[:, bass.ds(n * 4, 4), :], ps[7][:, 0:40].rearrange("p (a s) -> p a s", s=10)[:, :, 0:9],
                                  vec[:, bass.ds(n * 4, 4)].unsqueeze(2).broadcast_to([P, 4, 9]), ALU.add).then_inc(s_ada, 1)

            def ffn(which, base, b, gain, first, last, adas):
                if not first:
                    dve.wait_ge(s_xacc[which], b * 24)
                for u in range(3 * FB):
                    f, c = divmod(u, 3)
                    n = CHN[c]
                    dve.wait_ge(s_silu[which], b * 6 + (u + 1))
                    if not (first and u == 0):
                        dve.wait_ge(s_act[which], b * 6 + u)
                    dve.tensor_tensor(tb(7)[:, 0:n], tb(6)[:, 0:n], ps[2 * (u % 2) + 1][:, 0:n], ALU.mult).then_inc(s_a[which], 1)
                    dve.wait_ge(s_ahi[which], b * 6 + (u + 1))
                    dve.tensor_tensor(al[:, f, CH0[c]:CH0[c] + n], tb(7)[:, 0:n], ah[:, f, CH0[c]:CH0[c] + n].bitcast(F32),
                                      ALU.subtract).then_inc(s_act[which], 1)
                    if u == 0:
                        for t in (4, 5):
                            split_lo(b * 6 + (base + t), t % 3, wl[:, t, :], wh[:, t, :])
                    if u == 3 and not last:
                        for t in (0, 1):
                            split_lo(b * 6 + (base + 6 + t), t % 3, wl[:, t, :], wh[:, t, :])
                    if u == 4 and adas:
                        ada_sums(b + AU_FIRST)
                if not last:
                    for t in (2, 3):
                        split_lo(b * 6 + (base + 6 + t), t % 3, wl[:, t, :], wh[:, t, :])
                for c in range(NC):
                    for k in range(KT):
                        n = KT * c + k
                        dve.wait_ge(s_down[which], b * 24 + (n + 1))
                        add_residual(ps[4 + n % 3], k, c, gain, s_xacc[which])
                    if adas and c == 0:
                        ada_store(b + AU_FIRST)

            def ffn_all(which, base, gain, adas):
                ffn(which, base, 0, gain, True, False, adas)
                for_samples = (NB - 2)
                with dve.Fori(1, NB - 1) as b:
                    step.loop(b - 1, KT)
                    ffn(which, base, b, gain, False, False, adas)
                step.end_loop(for_samples)
                ffn(which, base, NB - 1, gain, False, True, adas)


            def core(c, tiles):
                for p in range(tiles):
                    t = 3 * c + p
                    w = NS if t == 8 else P
                    dve.wait_ge(g_kt, t + 1)
                    dve.tensor_copy(kdT[0:w, :], ps[6][0:w, 0:2 * P]).then_inc(g_kd, 1)
                    dve.wait_ge(g_at, t + 1)
                    dve.wait_ge(m_init, 2)
                    if t:
                        dve.wait_ge(g_o, t)
                    if t == 8:
                        step(dve.memset(attS[0:NS, :, 0:NS], 0.0))
                    mask = C_SM if t == 8 else C_CM
                    for a in range(w // GC):
                        r = slice(GC * a, GC * (a + 1))
                        for h2 in range(2):
                            ins = dve.copy_predicated(attS[r, h2:4:2, r],
                                                      cst[r, mask:mask + GC].bitcast(U32).unsqueeze(1).broadcast_to([GC, 2, GC]),
                                                      ps[h2][r, 0:2 * GC].rearrange("p (j n) -> p j n", j=2))
                    ins.then_inc(g_am, 1)
                    if t < 8:
                        for a in range(2):
                            g = 2 * t + a
                            dve.wait_ge(g_u, g + 1)
                            if g:
                                dve.wait_ge(g_s, g)
                            for j in range(2):
                                ins = dve.scalar_tensor_tensor(out=S[:, (g + 1) % 3, j, :], in0=S[:, g % 3, j, :],
                                                               scalar=dec[:, j, 2 * p + a:2 * p + a + 1],
                                                               in1=ps[4 + a][:, P * j:P * (j + 1)], op0=ALU.mult, op1=ALU.add)
                            ins.then_inc(g_s, 1)
                    dve.wait_ge(g_y, t + 1)
                    if t:
                        dve.wait_ge(g_lo, 2 * t)
                    q4 = 4 * w
                    V, Y, T3, R = (tmp[:, b:b + q4] for b in (1536, 1024, 2048, 2560))
                    dve.tensor_scalar(V, ps[7][:, 0:q4], 1.0 / DV, EPS, ALU.mult, ALU.add)
                    step(dve.tensor_tensor(T3, Y, Y, ALU.mult))
                    step(dve.scalar_tensor_tensor(out=T3, in0=T3, scalar=-0.5, in1=V, op0=ALU.mult, op1=ALU.mult))
                    step(dve.scalar_tensor_tensor(out=R, in0=T3, scalar=1.5, in1=Y, op0=ALU.add, op1=ALU.mult))

                    def half(b, h2):
                        return tmp[:, b + 2 * w * h2:b + 2 * w * (h2 + 1)].rearrange("p (j n) -> p j n", j=2)

                    for h2 in range(2):
                        ins = dve.scalar_tensor_tensor(out=half(1536, h2), in0=ps[2 + h2][:, 0:2 * P].rearrange("p (j n) -> p j n", j=2)[:, :, 0:w],
                                                       scalar=vec[:, R_GN:R_GN + 1], in1=half(2560, h2), op0=ALU.mult, op1=ALU.mult)
                    ins.then_inc(g_w, 1)
                    dve.wait_ge(g_w, t + 1)
                    dve.wait_ge(m_ev, NPROJ * (c + 1))
                    for h2 in range(2):
                        ins = dve.tensor_tensor(half(2048, h2), half(1536, h2), og[:, h2:4:2, P * p:P * p + w], ALU.mult)
                    ins.then_inc(g_f, 1)
                    dve.wait_ge(g_hi, t + 1)
                    for h2 in range(2):
                        z = (slice(None), slice(4 + h2, 8, 2), slice(P * t, P * t + w))
                        dve.tensor_tensor(hl[z], half(2048, h2), hh[z].bitcast(F32), ALU.subtract).then_inc(g_lo, 1)
                    if t == 8:
                        for s in range(NSEQ):
                            if s >= 2:
                                dve.wait_ge(g_su, s - 1)
                            dve.tensor_scalar(kx[:, 256 * (s % 2):256 * (s % 2 + 1)], kdT[0:NS, :],
                                              cst[0:NS, C_SEQ + s:C_SEQ + s + 1], None, ALU.mult).then_inc(g_kx, 1)
                            if s:
                                sample_state(s - 1)
                        sample_state(NSEQ - 1)

            def sample_state(s):
                dve.wait_ge(g_su, s + 1)
                for j in range(2):
                    ins = dve.scalar_tensor_tensor(out=S0[:, j, s, :], in0=S0[:, j, s, :], scalar=dec[:, j, 4 + s:5 + s],
                                                   in1=ps[4 + s % 2][:, P * j:P * (j + 1)], op0=ALU.mult, op1=ALU.add)
                ins.then_inc(g_s0, 1)

            dve.wait_ge(s_tr, 1)
            step(dve.tensor_copy(vec[:, 0:R_END], ps[0][:, 0:R_END]))
            for t in range(9):
                n = P if t < 8 else NS
                for a in range(2):
                    dve.wait_ge(s_tr, 3 + 2 * t + a)
                    dve.tensor_copy(xT[:, 4 * a:4 * a + 4, P * t:P * t + n],
                                    ps[2 + (2 * t + a) % 4][:, 0:4 * n].rearrange("p (k n) -> p k n", k=4)).then_inc(s_trev, 1)
            for u in range(AU_FIRST):
                ada_sums(u)
                ada_store(u)
            dve.wait_ge(s_ada, AU_FIRST)

            def norm_coef(q, scale_vec, row):
                step(dve.scalar_tensor_tensor(out=coef[:, q, :, :], in0=ada[:, scale_vec * KT:(scale_vec + 1) * KT, :], scalar=1.0,
                                              in1=vec[:, row:row + KT].unsqueeze(2).broadcast_to([P, KT, 9]), op0=ALU.add, op1=ALU.mult))

            def half_gain(v):
                a = ada[:, v * KT:(v + 1) * KT, :]
                step(dve.tensor_scalar(a, a, 0.5, None, ALU.mult))

            norm_coef(0, 1, R_LN1)
            half_gain(2)
            norm(0, 0)
            for t in range(4):
                split_lo(t, t % NWS, wl[:, t, :], wh[:, t, :])
            norm(1, 1)
            norm(2, 2)
            ffn_all(0, W_F1, 2 * KT, True)

            dve.wait_ge(s_ada, NAU)
            norm_coef(1, 4, R_LNM)
            norm_coef(2, 7, R_LN2)
            half_gain(8)
            for g in range(2):
                split_lo(W_MIX + g, g % NWS, mwl[:, g, :], mwh[:, g, :])
            dve.wait_ge(s_xacc[0], 24 * NB)
            norm(3, 0)
            for c in range(NC):
                n = CHN[c]
                m = n if c < 2 else LASTP
                nc_ = m // GC
                tiles = PAIRS[c] + (c == 2)

                def chunks(tensor, a):
                    if a == 0:
                        return tensor[:, :, 0:m].rearrange("p j (c t) -> p j c t", t=GC)
                    return tensor[:, :, m:n].rearrange("p j (c t) -> p j c t", t=TSEQ)

                for u in range(UPC):
                    g = UPC * c + u
                    if u == NPROJ:
                        core(c, tiles)
                    dve.wait_ge(m_unit, g + 1)
                    if g + 2 < UPC * NC:
                        split_lo(W_MIX + g + 2, (g + 2) % NWS, mwl[:, g % 2, :], mwh[:, g % 2, :])
                    elif g + 2 == UPC * NC:
                        for t in range(4):
                            split_lo(W_F2 + t, t % NWS, wl[:, t, :], wh[:, t, :])
                    if c == 0 and u < 2:
                        norm(4 + u, 1 + u)
                    if c == 2 and u == 0:
                        dve.wait_ge(m_buf, 1)
                        dve.wait_ge(m_z, 8)
                        for gg in range(4):
                            ins = dve.tensor_copy(sample_rows(gg)[:, :, 0:HALO],
                                                  ps[6][:, 120 * gg:120 * (gg + 1)].rearrange("p (s r) -> p s r", r=HALO))
                        ins.then_inc(m_bufc, 1)
                    if u == 4:
                        dve.wait_ge(m_pa, 4 * c + 1)
                        for j in range(2):
                            ins = dve.tensor_scalar(bs[:, j, 0:n], ps[6 + j][:, 0:n], vec[:, R_BGK + j:R_BGK + j + 1], 0.0, ALU.add, ALU.min)
                            ins.then_inc(m_gkr, 1)
                        dve.wait_ge(m_gkr, 2 * (c + 1))
                        step(dve.tensor_tensor(bs[:, :, 0:n], bs[:, :, 0:n], t1[:, :, 0:n], ALU.subtract))
                        for j in range(2):
                            ins = dve.tensor_tensor_scan(bs[:, j, 0:m], cst[:, C_RM:C_RM + m], bs[:, j, 0:m], 0.0, ALU.mult, ALU.add)
                            if c == 2:
                                ins = dve.tensor_tensor_scan(bs[:, j, m:n], cst[:, C_RM + CMAX:C_RM + CMAX + NS], bs[:, j, m:n],
                                                             0.0, ALU.mult, ALU.add)
                        step(ins)
                        ins = dve.tensor_copy(bl[:, :, 0:nc_], chunks(bs, 0)[:, :, :, GC - 1])
                        if c == 2:
                            ins = dve.tensor_copy(bl[:, :, nc_:nc_ + NSEQ], chunks(bs, 1)[:, :, :, TSEQ - 1])
                        elif c == 0:
                            step(dve.memset(bl[:, :, nc_:12], 0.0))
                            ins = dve.tensor_copy(bl[:, :, 0:nc_], chunks(bs, 0)[:, :, :, GC - 1])
                        ins.then_inc(m_pd, 1)
                    if u == 5:
                        dve.wait_ge(m_pa, 4 * c + 2)
                        dve.wait_ge(m_ev, NPROJ * c + IDX["q", 1] + 1)
                        dve.scalar_tensor_tensor(out=qs[:, :, 0:n], in0=qs[:, :, 0:n], scalar=DK ** -0.5, in1=t1[:, :, 0:n],
                                                 op0=ALU.mult, op1=ALU.mult).then_inc(m_pd, 1)
                    if u == 6:
                        dve.wait_ge(m_pa, 4 * c + 3)
                        ins = dve.tensor_tensor(chunks(bs, 0), bl[:, :, 0:nc_].unsqueeze(3).broadcast_to([P, 2, nc_, GC]), chunks(bs, 0), ALU.subtract)
                        if c == 2:
                            ins = dve.tensor_tensor(chunks(bs, 1), bl[:, :, nc_:nc_ + NSEQ].unsqueeze(3).broadcast_to([P, 2, NSEQ, TSEQ]),
                                                    chunks(bs, 1), ALU.subtract)
                        ins.then_inc(m_pd, 1)
                    if u == 7:
                        dve.wait_ge(m_pa, 4 * c + 4)
                        step(dve.tensor_tensor(bs[:, :, 0:n], bs[:, :, 0:n], ks[:, :, 0:n], ALU.mult))
                        dve.tensor_tensor(ks[:, :, 0:n], ks[:, :, 0:n], t1[:, :, 0:n], ALU.mult).then_inc(m_pd, 1)
                    if 7 <= u < 11:
                        h = u - 7
                        dve.wait_ge(m_vt, 4 * c + h + 1)
                        full = m // P
                        src = ps[6 + h % 2]
                        ins = dve.tensor_copy(vs[:, 0:full, DV * h:DV * (h + 1)], src[:, 0:P * full].rearrange("p (t e) -> p t e", e=P))
                        if c == 2:
                            dve.memset(vs[NS:P, full, DV * h:DV * (h + 1)], 0.0)
                            ins = dve.tensor_copy(vs[0:NS, full, DV * h:DV * (h + 1)], src[0:NS, P * full:P * (full + 1)])
                        ins.then_inc(m_vc, 1)
                    if c == 2 and u == 14:
                        dve.wait_ge(m_ut, 1)
                        dve.tensor_copy(rows[0:HALO, :], ps[6][0:HALO, :]).then_inc(m_uc, 1)
                        dve.wait_ge(m_ut, 2)
                        dve.tensor_copy(rows[NS:2 * NS, :], ps[7][0:NS, :]).then_inc(m_uc, 1)
                    if 14 <= u < NPROJ:
                        for gg in ((0,), (1,), (2, 3))[u - 14]:
                            dve.wait_ge(m_win, 4 * c + gg + 1)
                            W = HALO + m if c < 2 else EW
                            T = (TA, TB)[gg % 2]
                            dve.scalar_tensor_tensor(out=E[:, gg, HALO:W], in0=T[:, HALO:W], scalar=1.0 / PW[gg], in1=E[:, gg, HALO:W],
                                                     op0=ALU.mult, op1=ALU.subtract).then_inc(m_p, 1)
                    if u == NPROJ - 1:
                        for gg in range(4):
                            dve.wait_ge(m_zh, 4 * c + gg + 1)
                            z = slice(CH0[c], CH0[c] + n)
                            dve.scalar_tensor_tensor(out=hl[:, gg, z], in0=ps[gg][:, 0:n], scalar=vec[:, R_PS + gg:R_PS + gg + 1],
                                                     in1=hh[:, gg, z].bitcast(F32), op0=ALU.mult, op1=ALU.subtract).then_inc(m_zs, 1)
                    if u >= NPROJ:
                        k = u - NPROJ
                        add_residual(ps[k % RING], k, c, 5 * KT, m_x)
            dve.wait_ge(m_x, KT * NC)
            for q in range(6, 9):
                norm(q, q - 6)
            ffn_all(1, W_F2, 8 * KT, False)

            dve.wait_ge(s_lnf, 16)
            for t in range(9):
                w = P if t < 8 else NS
                r = rsf[0:w, t, :]
                dve.wait_ge(s_fy, t + 1)
                step(dve.tensor_scalar(r[:, 5:6], r[:, 2:3], 1.0 / D, EPS, ALU.mult, ALU.add))
                step(dve.tensor_tensor(r[:, 6:7], r[:, 4:5], r[:, 4:5], ALU.mult))
                step(dve.scalar_tensor_tensor(out=r[:, 6:7], in0=r[:, 6:7], scalar=-0.5, in1=r[:, 5:6], op0=ALU.mult, op1=ALU.mult))
                step(dve.scalar_tensor_tensor(out=r[:, 7:8], in0=r[:, 6:7], scalar=1.5, in1=r[:, 4:5], op0=ALU.add, op1=ALU.mult))
                if t >= 2:
                    dve.wait_ge(s_out[t % 2], 16 * (t // 2))
                for a in range(2):
                    ins = dve.scalar_tensor_tensor(out=yst[0:w, t % 2, 512 * a:512 * (a + 1)], in0=ps[2 * (t % 2) + a][0:w, :],
                                                   scalar=r[:, 7:8], in1=lnf[0:w, 512 * a:512 * (a + 1)], op0=ALU.mult, op1=ALU.mult)
                ins.then_inc(s_fo, 1)


_INS = ("x_prompt", "x_sample", "state_pool", "state_gla", "c_prompt", "c_sample", "ln_ffn1", "ln_mix", "ln_ffn2", "w_ada", "b_ada",
        "w_ffn1_up", "w_ffn1_down", "w_in", "w_gk2", "b_gk2", "w_pool", "pool_scale", "gla_norm", "w_out", "w_ffn2_up",
        "w_ffn2_down", "ln_final")
_LAYER = ("w_ada", "w_ffn1_up", "w_ffn1_down", "w_in", "w_gk2", "w_pool", "w_out", "w_ffn2_up", "w_ffn2_down")
_OUTS = (("y_p", (1, SEQ, D)), ("y_s", (NSEQ, TSEQ, D)), ("pool_p", (1, 1, HALO, 512)), ("gla_p", (1, 1, HEADS, DK, DV)),
         ("pool_s", (1, NSEQ, HALO, 512)), ("gla_s", (1, NSEQ, HEADS, DK, DV)))


def kernel(**inputs):
    import concourse.bacc as _bacc
    from concourse.bass_utils import run_bass_kernel_spmd as _run

    nc = _bacc.Bacc("TRN2", target_bir_lowering=False, num_devices=1)
    arrays, i, o = {}, {}, {}
    for name in _INS + ("const",):
        a = constants() if name == "const" else np.ascontiguousarray(inputs[name])
        if name in _LAYER:
            a = a[0]
        arrays[f"in_{name}"] = a
        i[name] = nc.dram_tensor(f"in_{name}", a.shape, F32, kind="ExternalInput").ap()
    for name, shape in _OUTS:
        o[name] = nc.dram_tensor(f"out_{name}", shape, F32, kind="ExternalOutput").ap()
    program(nc, i, o)
    r = _run(nc, [arrays], core_ids=[0])
    return tuple(r.results[0][f"out_{name}"] for name, _ in _OUTS)
```

```python
from contextlib import ExitStack

import numpy as np

import concourse.bass as bass
from concourse import mybir

F32 = mybir.dt.float32
F32R = mybir.dt.float32r
U32 = mybir.dt.uint32
ALU = mybir.AluOpType
ACT = mybir.ActivationFunctionType

P = 128
D = 1024
KT = D // P
SEQ = 1024
NSEQ, TSEQ = 8, 8
NS = NSEQ * TSEQ
TOK = SEQ + NS
F = 2816
NF = F // P
FB = 2
NB = NF // FB
CH0 = (0, 384, 768)
CHN = (384, 384, 320)
NC = 3
CMAX = 384
LASTP = CHN[2] - NS
HEADS, DK, DV = 4, 64, 128
GC = 64
PW = (2, 4, 8, 16)
HALO = 15
EW = HALO + LASTP + NSEQ * (HALO + TSEQ)
SB = HALO + LASTP
SW = HALO + TSEQ
EPS = 1e-6
NADA = 9
AU = 512
NAU = NADA * D // AU
AU_FIRST = NAU - NB
V_U, V_Q, V_K, V_V, V_GLR, V_OG = 0, 512, 768, 1024, 1536, 1552

PROJ = ([("glr", 0, V_GLR)] + [("k", j, V_K + P * j) for j in range(2)] + [("q", j, V_Q + P * j) for j in range(2)]
        + [("v", j, V_V + P * j) for j in range(4)] + [("og", j, V_OG + P * j) for j in range(4)]
        + [("u", j, V_U + P * j) for j in range(4)])
NPROJ = len(PROJ)
WSTART = 5
UNITS = []
for _c in range(NC):
    UNITS += [("p", _c, _u) for _u in range(WSTART)]
    UNITS += [("w", _c - 1, _k) for _k in range(KT)] if _c else []
    UNITS += [("p", _c, _u) for _u in range(WSTART, NPROJ)]
UNITS += [("w", NC - 1, _k) for _k in range(KT)]
NU = len(UNITS)
_w = [[("p", _c, 3), ("p", _c, 4)] + [("w", _c - 1, _k) for _k in range(7)] for _c in range(NC)]
_p = [("p", 0, _u) for _u in range(10)]
NORMS = {4: (1, _p[:4], _p[5], _p[6:]), 5: (2, _w[1][:4], _w[1][4], _w[1][5:]), 6: (0, _w[2][:4], _w[2][4], _w[2][5:]),
         7: (1, [("w", 1, 7), ("p", 2, 5)], ("p", 2, 7), [("p", 2, _u) for _u in range(8, 12)])}
LAST_NORM = (4, 5, 7)
CORE = {10: "K0", 11: "U0", 12: "O0 K1", 13: "U1 Q0", 14: "O1 K2", 15: "U2 Q1", 16: "O2"}
IDX = {(kind, j): i for i, (kind, j, _) in enumerate(PROJ)}
RING = 3
W_F1, W_MIX, W_F2 = 0, NB * 6, NB * 6 + NU
NWS = 3
NYST = 4
NX = 9
LATE = (0, 3, 6, KT)
PAIRS = (3, 3, 2)

R_BADA, R_LN1, R_LNM, R_LN2, R_BGK, R_PS, R_GN, R_END = 0, 72, 80, 88, 96, 98, 102, 103
C_ID, C_RM, C_RATIO, C_CM, C_SM, C_SEQ, C_SEL, C_END = 0, 128, 576, 636, 700, 764, 772, 782


def constants():
    c = np.zeros((P, C_END), np.float32)
    c[:, C_ID:C_ID + P] = np.eye(P)
    c[:, C_RM:C_RM + CMAX] = (np.arange(CMAX) % GC != 0)
    c[:, C_RM + CMAX:C_RM + CMAX + NS] = (np.arange(NS) % TSEQ != 0)
    for g, w in enumerate(PW):
        c[:, C_RATIO + HALO * g:C_RATIO + HALO * (g + 1)] = w / np.minimum(np.arange(HALO) + 1, w)
    s, t = np.arange(P)[:, None] % GC, np.arange(GC)[None]
    c[:, C_CM:C_CM + GC] = s <= t
    c[:, C_SM:C_SM + GC] = (s <= t) & (s // TSEQ == t // TSEQ)
    c[:, C_SEQ:C_SEQ + NSEQ] = s // TSEQ == np.arange(NSEQ)[None]
    c[:, C_SEL:C_SEL + 10] = np.arange(P)[:, None] % 32 == np.arange(10)[None]
    return c


class Steps:

    def __init__(self, eng, sem):
        self.eng, self.sem, self.n, self.base, self.start = eng, sem, 0, None, 0

    def loop(self, i, per):
        self.base, self.start, self.per = i * per, self.n, per

    def end_loop(self, trips):
        assert self.n - self.start == self.per, (self.n - self.start, self.per)
        self.n = self.start + self.per * trips
        self.base = None

    def __call__(self, ins):
        self.n += 1
        ins.then_inc(self.sem, 1)
        self.eng.wait_ge(self.sem, self.n if self.base is None else self.base + self.n)


def program(nc, i, o):
    es = ExitStack()

    def sem(name):
        return es.enter_context(nc.semaphore(name))

    def sb(name, shape, dt=F32, ctx=es):
        return ctx.enter_context(nc.sbuf_tensor(name, shape, dt))

    with es:
        xT = sb("xT", [P, KT, TOK])
        with ExitStack() as start_ada:
            ai = sb("ai", [P, 4, KT, AU], F32, start_ada)
        hh = sb("hh", [P, KT, TOK], F32R)
        hl = sb("hl", [P, KT, TOK], F32R)
        ws = sb("ws", [P, NWS, 1024])
        tmp = sb("tmp", [P, 8 * CMAX])
        cst = sb("cst", [P, C_END])
        ones = sb("ones", [P, P])
        vec = sb("vec", [P, R_END + 1])
        ada = sb("ada", [P, NADA * KT, 9])
        coef = sb("coef", [P, 3, KT, 9])

        def tb(k):
            return tmp[:, k * CMAX:(k + 1) * CMAX]

        with ExitStack() as ffn:
            wh = sb("wh", [P, 6, 1024], F32R, ffn)
            wl = sb("wl", [P, 6, 1024], F32R, ffn)
            ah = sb("ah", [P, FB, TOK], F32R, ffn)
            al = sb("al", [P, FB, TOK], F32R, ffn)
            with ExitStack() as first:
                aws = sb("aws", [P, 2, AU], F32, first)
                csT = sb("csT", [P, KT, 32], F32, first)
                aev = sb("aev", [P, AU], F32, first)
            with ExitStack() as last:
                lnf = sb("lnf", [P, D], F32, last)
                rsf = sb("rsf", [P, 9, 8], F32, last)
        with ExitStack() as start:
            xin = sb("xin", [P, NX // 3, D], F32, start)
            vin = sb("vin", [R_END, P], F32, start)
            cin = sb("cin", [9, D], F32, start)
            ai2 = sb("ai2", [P, AU_FIRST - 4, KT, AU], F32, start)
        with ExitStack() as end:
            yst = sb("yst", [P, NYST, D], F32, end)
        with ExitStack() as mix:
            qs = sb("qs", [P, 2, CMAX], F32, mix)
            ks = sb("ks", [P, 2, CMAX], F32, mix)
            bs = sb("bs", [P, 2, CMAX], F32, mix)
            t1 = sb("t1", [P, 2, CMAX], F32, mix)
            vs = sb("vs", [P, 3, 512], F32, mix)
            og = sb("og", [P, 4, CMAX], F32, mix)
            E = sb("E", [P, 4, EW], F32, mix)
            attS = sb("attS", [P, 4, P], F32, mix)
            S = sb("S", [P, 3, 2, DV], F32, mix)
            S0 = sb("S0", [P, 2, NSEQ, DV], F32, mix)
            mwh = sb("mwh", [P, 2, 1024], F32R, mix)
            mwl = sb("mwl", [P, 2, 1024], F32R, mix)
            kdT = sb("kdT", [P, 2 * P], F32, mix)
            rows = sb("rows", [P, 512], F32, mix)
            TA = sb("TA", [P, EW], F32, mix)
            TB = sb("TB", [P, EW], F32, mix)
            wp = sb("wp", [P, 4, P], F32, mix)
            wg = sb("wg", [16, 2 * P], F32, mix)
            halo = sb("halo", [P, 4, HALO], F32, mix)
            vtmp = sb("vtmp", [P, CMAX], F32, mix)
            bl = sb("bl", [P, 2, 12], F32, mix)
            dec = sb("dec", [P, 2, 12], F32, mix)
        glr = vtmp
        kx = t1[0:NS, :, :].rearrange("p j n -> p (j n)")

        ps = [es.enter_context(nc.psum_tensor(f"bank{b}", [P, 512], F32)) for b in range(8)]

        s_x = [sem(f"x_loaded{k}") for k in range(NX)]; s_ai = [sem(f"first_ada_weights{k}") for k in range(AU_FIRST)]
        s_cst = sem("constants_loaded"); s_small = sem("small_loaded"); s_ones = sem("ones_set")
        s_tr = sem("pe_start_transposes"); s_trev = sem("start_transposes_copied")
        s_cs = sem("silu_c_ready")
        s_aw = [sem(f"ada_weights_loaded{k}") for k in range(2)]
        s_apc = sem("ada_piece_used"); s_apf = sem("first_ada_sums"); s_asel = sem("ada_selected"); s_aevc = sem("ada_sums_copied")
        s_ada = sem("ada_unit_stored"); s_coef = sem("norm_coefficients")
        s_ws = [sem(f"weight_loaded{k}") for k in range(NWS)]
        s_whi = sem("weight_high"); s_wsp = sem("weight_split")
        s_up = [sem("up_done1"), sem("up_done2")]; s_down = [sem("down_done1"), sem("down_done2")]
        s_silu = [sem("silu1"), sem("silu2")]; s_a = [sem("act_product1"), sem("act_product2")]
        s_ahi = [sem("act_high1"), sem("act_high2")]; s_act = [sem("act_split1"), sem("act_split2")]
        s_xacc = [sem("residual1"), sem("residual2")]
        n_sq = sem("norm_square"); n_add = sem("norm_added"); n_ss = sem("norm_sum")
        n_ln = sem("norm_log"); g_ln = sem("gla_log"); n_y = sem("norm_rsqrt"); n_v = sem("norm_rsqrt_refined"); n_yk = sem("norm_scaled"); n_hi = sem("norm_high"); n_lo = sem("norm_split")
        s_dve = sem("dve_step"); s_acts = sem("act_step"); s_pool = sem("pool_step")
        m_ld = sem("mix_inputs_loaded"); m_unit = sem("mix_unit_done"); m_ev = sem("proj_copied")
        m_gk = sem("gate_logits"); m_gkr = sem("gate_logits_read")
        m_pa = sem("prep_by_act"); m_pd = sem("prep_by_dve")
        m_vt = sem("v_turned"); m_vc = sem("v_copied")
        m_buf = sem("pool_buffers_turned"); m_bufc = sem("pool_buffers_copied")
        m_win = sem("window_sum"); m_p = sem("pooled"); m_z = sem("z_product"); m_zh = sem("z_high"); m_zs = sem("z_split")
        m_ut = sem("u_turned"); m_uc = sem("u_rows_copied"); m_ust = sem("u_rows_stored")
        m_init = sem("mix_zeroed")
        g_at = sem("keys_turned_and_scores"); g_am = sem("scores_masked")
        g_u = sem("state_update"); g_s = sem("state_ready"); g_o = sem("gla_out"); g_sq = sem("gla_square")
        g_ss = sem("gla_sum"); g_y = sem("gla_rsqrt"); g_w = sem("gla_scaled"); g_f = sem("gla_gated"); g_hi = sem("gla_high"); g_lo = sem("gla_split")
        g_kx = sem("masked_keys"); g_su = sem("sample_update"); g_s0 = sem("sample_state")
        m_x = sem("mix_residual"); m_st = sem("states_stored")
        s_ft = sem("final_turned"); s_fsq = sem("final_squares"); s_fl = sem("final_mean"); s_fy = sem("final_rsqrt"); s_fo = sem("final_scaled")
        s_out = [sem(f"y_stored{k}") for k in range(NYST)]; s_lnf = sem("ln_final_loaded"); s_cp = sem("pool_rows_passed")

        block = es.enter_context(nc.Block())
        ident = cst[:, C_ID:C_ID + P]

        def sample_rows(g):
            return E[:, g, SB:SB + NSEQ * SW].rearrange("p (s w) -> p s w", w=SW)

        def sample_u(g):
            return sample_rows(g)[:, :, HALO:SW]

        def seqs(ap):
            return ap.rearrange("p (s t) -> p s t", t=TSEQ)

        def norm_bank(q):
            return ps[7] if q >= 3 else ps[4 + q]

        def x_rows(t):
            if t < 3:
                return xin[:, t, :]
            return ws[:, t - 3, :] if t < 6 else tmp[:, D * (t - 6):D * (t - 5)]

        def square(q, k):
            return tb(6 + k % 2) if q < 3 else tb((0, 1, 3, 4)[k % 4])

        def turned(t, a):
            return ps[2 * (t if t < 2 else (t - 2) % 4) + a]

        def cols(w, c0):
            return w[:, c0:c0 + P].rearrange("(k p) n -> p k n", p=P)

        def unit_of(u, by_chunk):
            return (u % FB, u // FB) if by_chunk else divmod(u, NC)

        def block_order(which, last):
            return (0, 1, 2, -1, 3, 4, -2, 5, -3) if which == 0 and last else (0, 1, 2, 3, 4, 5, -1, -2, -3)

        def ada_unit(u):
            return i["w_ada"][:, AU * u:AU * (u + 1)].rearrange("(k p) n -> p k n", p=P)

        @block.sync
        def _(sp):
            sp.dma_start(cst[:, :], i["const"]).then_inc(s_cst, 16)
            for t in range(NX):
                src = i["x_prompt"][0, P * t:P * (t + 1), :] if t < 8 else i["x_sample"].rearrange("b t d -> (b t) d")
                sp.dma_start(x_rows(t)[0:P if t < 8 else NS, :], src).then_inc(s_x[t], 16)
            for u in range(4):
                sp.dma_start(ai[:, u, :, :], ada_unit(u)).then_inc(s_ai[u], 16)

            def load_w(n, slot, src):
                if not isinstance(n, int) or n >= NWS:
                    sp.wait_ge(s_wsp, n - NWS + 1)
                sp.dma_start(ws[:, slot, :].rearrange("p (k n) -> p k n", n=P) if len(src.shape) == 3 else ws[:, slot, :],
                             src).then_inc(s_ws[slot], 16)

            def load_ada(n, slot, src):
                if not isinstance(n, int) or n >= 2:
                    sp.wait_ge(s_apc, n - 1)
                sp.dma_start(aws[:, slot, :], src).then_inc(s_aw[slot], 16)

            def ffn_tiles(up, down, base, b, adas=None):
                srcs = []
                for f in range(FB):
                    for half in range(2):
                        c0 = b * (FB * P) + (F * half + P * f)
                        srcs.append(up[:, bass.ds(c0, P)].rearrange("(k p) n -> p k n", p=P))
                for f in range(FB):
                    srcs.append(down[bass.ds(b * (FB * P) + P * f, P), :])
                for t, src in enumerate(srcs):
                    load_w(b * 6 + (base + t), (base + t) % NWS, src)
                    if adas == "start" and t == NWS - 1:
                        for u in range(4, AU_FIRST):
                            sp.dma_start(ai2[:, u - 4, :, :], ada_unit(u)).then_inc(s_ai[u], 16)
                        sp.dma_start(o["pool_s"][0, :, 0:HALO - TSEQ, :], i["state_pool"][0, :, TSEQ:HALO, :]).then_inc(s_cp, 16)
                if adas is not None:
                    for k in range(KT):
                        load_ada(b * KT + k, k % 2,
                                 i["w_ada"][P * k:P * (k + 1), bass.ds(b * AU + AU_FIRST * AU, AU)])

            sp.wait_ge(s_tr, 2 * 6)
            ffn_tiles(i["w_ffn1_up"], i["w_ffn1_down"], W_F1, 0, "start")
            with sp.Fori(1, NB) as b:
                ffn_tiles(i["w_ffn1_up"], i["w_ffn1_down"], W_F1, b, True)
            for g, (kind, c, u) in enumerate(UNITS):
                if g == NU - 3:
                    sp.wait_ge(m_uc, 1)
                    sp.dma_start(o["pool_p"][0, 0, :, :], rows[0:HALO, :]).then_inc(m_ust, 16)
                    sp.wait_ge(m_uc, 2)
                    sp.dma_start(o["pool_s"][0, :, HALO - TSEQ:HALO, :], rows[NS:2 * NS, :]).then_inc(m_ust, 16)
                    sp.wait_ge(g_s, 16)
                    for j in range(2):
                        sp.dma_start(o["gla_p"][0, 0, 2 * j:2 * j + 2, :, :].rearrange("h d e -> (h d) e"),
                                     S[:, 16 % 3, j, :]).then_inc(m_st, 16)
                load_w(W_MIX + g, (W_MIX + g) % NWS, cols(i["w_in"], PROJ[u][2]) if kind == "p" else cols(i["w_out"], P * u))
                if g == NWS - 1:
                    sp.wait_ge(s_down[0], 24 * NB)
                    sp.wait_ge(s_act[0], 6 * NB)
                    sp.dma_start(wg[:, :], i["w_gk2"]).then_inc(m_ld, 16)
                    sp.dma_start(wp[:, :, :], i["w_pool"].rearrange("g p n -> p g n")).then_inc(m_ld, 16)
                    sp.dma_start(rows[0:NSEQ * HALO, :], i["state_pool"].rearrange("a b r d -> (a b r) d")).then_inc(m_ld, 16)
                    for j in range(2):
                        sp.dma_start(S0[:, j, :, :], i["state_gla"][0, :, 2 * j:2 * j + 2, :, :]
                                     .rearrange("s h d e -> (h d) s e")).then_inc(m_ld, 16)
            sp.wait_ge(g_s0, NSEQ)
            for j in range(2):
                sp.dma_start(o["gla_s"][0, :, 2 * j:2 * j + 2, :, :].rearrange("s h d e -> (h d) s e"),
                             S0[:, j, :, :]).then_inc(m_st, 16)
            sp.wait_ge(s_down[0], 24 * NB)
            ffn_tiles(i["w_ffn2_up"], i["w_ffn2_down"], W_F2, 0)
            with sp.Fori(1, NB) as b:
                ffn_tiles(i["w_ffn2_up"], i["w_ffn2_down"], W_F2, b)
            sp.dma_start(lnf[:, :], i["ln_final"].rearrange("(a d) -> a d", a=1).broadcast_to([P, D])).then_inc(s_lnf, 16)
            yp = o["y_p"][0].rearrange("(t p) d -> t p d", p=P)
            for t in range(9):
                sp.wait_ge(s_fo, t + 1)
                if t < 8:
                    sp.dma_start(yp[t], yst[:, t % NYST, :]).then_inc(s_out[t % NYST], 16)
                else:
                    sp.dma_start(o["y_s"].rearrange("b t d -> (b t) d"), yst[0:NS, t % NYST, :]).then_inc(s_out[t % NYST], 16)
            for k in range(NYST):
                sp.wait_ge(s_out[k], 16 * len(range(k, NX, NYST)))
            sp.wait_ge(m_ust, 32)
            sp.wait_ge(m_st, 64)
            sp.wait_ge(s_cp, 16)

        @block.tensor
        def _(pe):
            def split_product(out, w_hi, w_lo, x_hi, x_lo, depth, x_ready=None):
                for k in range(depth):
                    if x_ready is not None:
                        pe.wait_ge(n_lo, x_ready + k + 1)
                    for a, (l, r) in enumerate(((w_hi, x_hi), (w_hi, x_lo), (w_lo, x_hi))):
                        mm = pe.matmul(out, l(k), r(k), start=(k == 0 and a == 0), stop=(k == depth - 1 and a == 2))
                return mm

            def ada_rows(bank, k, w):
                q = k % 4
                return pe.matmul(bank[32 * q:32 * q + 32, :], csT[:, k, :], w, start=(k < 4), stop=(k >= 4))

            def ada_piece(n, k, slot):
                pe.wait_ge(s_aw[slot], n * 64 + 16 * (k // 2 + 1))
                ada_rows(ps[7], k, aws[:, slot, :]).then_inc(s_apc, 1)

            def ada_select(bank):
                for a in range(4):
                    mm = pe.matmul(bank[:, 10 * a:10 * a + 10], aev[:, P * a:P * (a + 1)], cst[:, C_SEL:C_SEL + 10],
                                   start=True, stop=True)
                mm.then_inc(s_asel, 1)

            def ones_sum(q, n):
                pe.wait_ge(n_add, KT * (q + 1))
                if q >= 4:
                    pe.wait_ge(n_v, q)
                pe.matmul(norm_bank(q)[:, 0:n], ones[:, :], tb(2)[:, 0:n], start=True, stop=True).then_inc(n_ss, 1)

            def ffn(which, base, b, q0, adas, first, last):
                whi = lambda s: (lambda k: wh[:, s, P * k:P * (k + 1)])
                wlo = lambda s: (lambda k: wl[:, s, P * k:P * (k + 1)])
                by_chunk = first or (which == 0 and last)

                def up(u):
                    f, c = unit_of(u, by_chunk)
                    sl = slice(CH0[c], CH0[c] + CHN[c])
                    if first and f == 0:
                        pe.wait_ge(n_lo, KT * (q0 + c + 1))
                    if c == 0:
                        pe.wait_ge(s_wsp, b * 6 + (base + 2 * f + 2))
                    if first and which == 1 and u == 1:
                        pe.wait_ge(m_x, KT * NC)
                        pe.wait_ge(g_s0, NSEQ)
                    if not (first and u < 2):
                        pe.wait_ge(s_a[which], b * 6 + (u - 1))
                    for half in range(2):
                        bank = ps[2 * (u % 2) + half][:, 0:CHN[c]]
                        s = 2 * f + half
                        mm = split_product(bank, whi(s), wlo(s), lambda k: hh[:, k, sl], lambda k: hl[:, k, sl], KT)
                    mm.then_inc(s_up[which], 1)
                    if first and which == 1 and u == 0:
                        ones_sum(q0 + 2, CHN[2])
                    if adas:
                        if u < 4:
                            if u == 0:
                                pe.wait_ge(s_ada, b + AU_FIRST)
                            ada_piece(b, 2 * u, 0)
                            ada_piece(b, 2 * u + 1, 1)

                def down(c):
                    if c == 0:
                        pe.wait_ge(s_wsp, b * 6 + (base + 6))
                    sl = slice(CH0[c], CH0[c] + CHN[c])
                    pe.wait_ge(s_act[which], b * 6 + (2 * c + 2 if which == 0 and last else 4 + c))
                    for m in range(KT):
                        n = KT * c + m
                        if not (first and n < 3):
                            pe.wait_ge(s_xacc[which], b * 24 + (n - 2))
                        split_product(ps[4 + n % 3][:, 0:CHN[c]], lambda k: wh[:, 4 + k, P * m:P * (m + 1)],
                                      lambda k: wl[:, 4 + k, P * m:P * (m + 1)], lambda k: ah[:, k, sl],
                                      lambda k: al[:, k, sl], FB).then_inc(s_down[which], 1)
                        if which == 1 and last and n == 20:
                            final_turn(2)
                        if which == 0 and last and n == 11:
                            pe.wait_ge(s_aevc, NAU)
                            ada_select(ps[7])
                        if which == 0 and last and n == 15:
                            pe.wait_ge(s_ada, NAU)
                            ones_sum(3, CHN[0])
                    if adas and c == 0 and not last:
                        pe.wait_ge(s_aevc, b + (AU_FIRST + 1))
                        ada_select(ps[7])
                    if which == 1 and last and c == 1:
                        final_turn(0)
                        final_turn(1)

                for what in block_order(which, last):
                    if what >= 0:
                        up(what)
                    else:
                        down(-1 - what)

            def final_turn(t):
                w = P if t < 8 else NS
                if t < 2:
                    pe.wait_ge(s_a[1], 6 * NB)
                elif t < 4:
                    pe.wait_ge(s_fo, t - 1)
                elif t >= 6:
                    pe.wait_ge(s_fo, t - 3)
                if t >= 4:
                    pe.wait_ge(s_xacc[1], 24 * NB)
                pe.wait_ge(s_xacc[1], 24 * (NB - 1) + KT * (t // 3 + 1))
                for k in range(KT):
                    mm = pe.transpose(turned(t, k // 4)[0:w, P * (k % 4):P * (k % 4 + 1)], xT[:, k, P * t:P * t + w], ident)
                mm.then_inc(s_ft, 1)

            pe.wait_ge(s_cst, 16)
            for t in range(NX):
                pe.wait_ge(s_x[t], 16)
                n = P if t < 8 else NS
                for a in range(2):
                    bank = 2 + (2 * t + a) % 4
                    if 2 * t + a >= 4:
                        pe.wait_ge(s_trev, 2 * t + a - 3)
                    for k in range(4):
                        mm = pe.transpose(ps[bank][:, n * k:n * k + n], x_rows(t)[0:n, P * (4 * a + k):P * (4 * a + k + 1)],
                                          cst[0:n, C_ID:C_ID + n])
                    mm.then_inc(s_tr, 1)
            pe.wait_ge(s_small, 16 * 9)
            pe.transpose(ps[0][:, 0:R_END], vin[:, :], cst[0:R_END, C_ID:C_ID + R_END]).then_inc(s_tr, 1)
            for k in range(KT):
                mm = pe.transpose(ps[1][:, 9 * k:9 * k + 9], cin[:, P * k:P * (k + 1)], cst[0:9, C_ID:C_ID + 9])
            mm.then_inc(s_tr, 1)
            pe.wait_ge(s_cs, 2)
            pe.wait_ge(s_ones, 1)
            pe.wait_ge(s_trev, 2 * NX)
            for u in range(AU_FIRST + 1):
                if u:
                    pe.wait_ge(s_aevc, u)
                    if u >= 2:
                        pe.wait_ge(s_ada, u - 1)
                    ada_select(ps[2])
                if u < AU_FIRST:
                    pe.wait_ge(s_ai[u], 16)
                    for k in range(KT):
                        mm = ada_rows(ps[7 - 4 * (u % 2)], k, ai[:, u, k, :] if u < 4 else ai2[:, u - 4, k, :])
                    mm.then_inc(s_apf, 1)
                if u in (2, 4):
                    ones_sum(u // 2 - 1, CHN[u // 2 - 1])
            ones_sum(2, CHN[2])
            ffn(0, W_F1, 0, 0, True, True, False)
            with pe.Fori(1, NB - 1) as b:
                ffn(0, W_F1, b, 0, True, False, False)
            ffn(0, W_F1, NB - 1, 0, True, False, True)

            pe.wait_ge(s_ada, NAU)

            def unit(g):
                kind, c, u = UNITS[g]
                pe.wait_ge(s_wsp, W_MIX + g + 1)
                if g >= RING:
                    before, cb, ub = UNITS[g - RING]
                    if before == "p":
                        pe.wait_ge(m_ev, NPROJ * cb + ub + 1)
                    else:
                        pe.wait_ge(m_x, KT * cb + ub + 1)
                s, sl = g % 2, slice(CH0[c], CH0[c] + CHN[c])
                split_product(ps[g % RING][:, 0:CHN[c]], lambda k: mwh[:, s, P * k:P * (k + 1)], lambda k: mwl[:, s, P * k:P * (k + 1)],
                              lambda k: hh[:, k, sl], lambda k: hl[:, k, sl], KT,
                              KT * (3 + c) if kind == "p" and u == 0 else None).then_inc(m_unit, 1)

            def turn_v(c, h):
                pe.wait_ge(m_ev, NPROJ * c + IDX["v", h] + 1)
                v = 4 * c + h
                if v >= 2:
                    pe.wait_ge(m_vc, v - 1)
                if h < 2:
                    pe.wait_ge(m_gkr, 2 * (c + 1))
                for t in range(PAIRS[c] + (c == 2)):
                    w = NS if c == 2 and t == 2 else P
                    mm = pe.transpose(ps[5 + h % 2][0:w, P * t:P * (t + 1)], vtmp[:, P * t:P * t + w], ident)
                mm.then_inc(m_vt, 1)

            def keys_scores(c, p):
                t = 3 * c + p
                w = NS if t == 8 else P
                cs = slice(P * p, P * p + w)
                if p == 0:
                    pe.wait_ge(m_pd, 4 * (c + 1))
                if t:
                    pe.wait_ge(g_s, 2 * t)
                for j in range(2):
                    pe.transpose(ps[3 + j][0:w, 3 * P:4 * P], bs[:, j, cs], ident)
                for h in range(HEADS):
                    r = slice(DK * (h % 2), DK * (h % 2) + DK)
                    for a in range(w // GC):
                        cc = slice(P * p + GC * a, P * p + GC * (a + 1))
                        mm = pe.matmul(ps[3 + h % 2][GC * a:GC * (a + 1), GC * (h // 2):GC * (h // 2 + 1)],
                                       ks[r, h // 2, cc], qs[r, h // 2, cc], start=True, stop=True)
                mm.then_inc(g_at, 1)

            def update(c, p):
                t = 3 * c + p
                pe.wait_ge(g_am, t + 1)
                pe.wait_ge(m_vc, 4 * (c + 1))
                for a in range(2):
                    for h in range(HEADS):
                        mm = pe.matmul(ps[3 + a][DK * (h % 2):DK * (h % 2) + DK, P * (1 + h // 2):P * (2 + h // 2)],
                                       kdT[GC * a:GC * (a + 1), DK * h:DK * (h + 1)],
                                       vs[GC * a:GC * (a + 1), p, DV * h:DV * (h + 1)], start=True, stop=True)
                    mm.then_inc(g_u, 1)

            def output(c, p):
                t = 3 * c + p
                w = NS if t == 8 else P
                pe.wait_ge(g_am, t + 1)
                pe.wait_ge(m_vc, 4 * (c + 1))
                if t:
                    pe.wait_ge(g_w, t)
                    pe.wait_ge(g_sq, t)
                if t < 8:
                    pe.wait_ge(g_s, 2 * t + 1)
                if t == 0:
                    pe.wait_ge(m_init, 2)
                for h in range(HEADS):
                    r = slice(DK * (h % 2), DK * (h % 2) + DK)
                    ob = ps[5 + h % 2][:, P * (h // 2):P * (h // 2) + w]
                    pe.matmul(ob, vs[:, p, DV * h:DV * (h + 1)], attS[:, h, 0:w], start=True, stop=False)
                    if t < 8:
                        for a in range(2):
                            mm = pe.matmul(ob[:, GC * a:GC * (a + 1)], S[r, (2 * t + a) % 3, h // 2, :],
                                           qs[r, h // 2, P * p + GC * a:P * p + GC * (a + 1)], start=False, stop=(a == 1))
                    else:
                        for s in range(NSEQ):
                            mm = pe.matmul(ob[:, TSEQ * s:TSEQ * (s + 1)], S0[r, h // 2, s, :],
                                           qs[r, h // 2, P * p + TSEQ * s:P * p + TSEQ * (s + 1)], start=False, stop=(s == NSEQ - 1))
                mm.then_inc(g_o, 1)

            def square_sum(c, p):
                t = 3 * c + p
                w = NS if t == 8 else P
                pe.wait_ge(g_sq, t + 1)
                pe.wait_ge(n_v, LAST_NORM[c] + 1)
                if t:
                    pe.wait_ge(g_f, t)
                if c == 2:
                    pe.wait_ge(m_bufc, 1)
                pe.matmul(ps[7][:, 0:4 * w], ones[:, :], tmp[:, 0:4 * w], start=True, stop=True).then_inc(g_ss, 1)

            def after(c, g):
                n = CHN[c]
                if g == 0:
                    square_sum(c, 2)
                if g < 2:
                    pe.wait_ge(g_am, 3 * c + 3)
                    pe.wait_ge(g_s, 2 * min(3 * c + 3, 8))
                else:
                    pe.wait_ge(m_zs, 4 * c + g - 1)
                pe.wait_ge(m_p, 4 * c + g + 1)
                np_ = n if c < 2 else LASTP
                mm = pe.matmul(ps[3 + g % 2][:, 0:np_], wp[:, g, :], E[:, g, HALO:HALO + np_], start=True, stop=True)
                if c == 2:
                    mm = pe.matmul(ps[3 + g % 2][:, np_:n], wp[:, g, :], sample_u(g), start=True, stop=True)
                mm.then_inc(m_z, 1)
                if c == 2 and g == 2:
                    pe.wait_ge(g_w, 9)
                    pe.wait_ge(g_sq, 9)
                    pe.wait_ge(m_win, 12)
                    pe.wait_ge(m_ev, NPROJ * NC)
                    for k in range(4):
                        mm = pe.transpose(ps[5][0:HALO, P * k:P * (k + 1)], halo[:, k, :], ident)
                    mm.then_inc(m_ut, 1)
                    for k in range(4):
                        mm = pe.transpose(ps[6][0:NS, P * k:P * (k + 1)], vtmp[:, NS * k:NS * (k + 1)], ident)
                    mm.then_inc(m_ut, 1)

            def sample_update(s):
                pe.wait_ge(g_kx, s + 1)
                if s >= 2:
                    pe.wait_ge(g_s0, s - 1)
                else:
                    pe.wait_ge(m_zs, 12)
                for h in range(HEADS):
                    mm = pe.matmul(ps[3 + s % 2][DK * (h % 2):DK * (h % 2) + DK, P * (h // 2):P * (h // 2 + 1)],
                                   kx[:, 256 * (s % 2) + DK * h:256 * (s % 2) + DK * (h + 1)],
                                   vs[0:NS, 2, DV * h:DV * (h + 1)], start=True, stop=True)
                mm.then_inc(g_su, 1)

            for g, (kind, c, u) in enumerate(UNITS):
                if kind == "w" and u == 0:
                    if c == 2:
                        for k in range(4):
                            after(2, k)
                    pe.wait_ge(m_zs, 4 * (c + 1))
                    pe.wait_ge(g_lo, c + 1)
                unit(g)
                for q, (nc_, _, s_sum, _) in NORMS.items():
                    if s_sum == (kind, c, u):
                        if q in (5, 6):
                            pe.wait_ge(g_f, 3 * (q - 4))
                        ones_sum(q, CHN[nc_])
                if kind == "w":
                    if c == 2 and u < NSEQ // 2:
                        sample_update(2 * u)
                        sample_update(2 * u + 1)
                    continue
                if c and u < 4:
                    after(c - 1, u)
                if u == 3:
                    if c == 0:
                        pe.wait_ge(m_ld, 16 * 5)
                        pe.wait_ge(s_xacc[0], 24 * NB)
                    else:
                        pe.wait_ge(g_w, 3 * c)
                        pe.wait_ge(g_sq, 3 * c)
                    pe.wait_ge(m_ev, NPROJ * c + 1)
                    for j in range(2):
                        pe.matmul(ps[5 + j][:, 0:CHN[c]], wg[:, P * j:P * (j + 1)], glr[0:16, 0:CHN[c]],
                                  start=True, stop=True).then_inc(m_gk, 1)
                if 6 <= u < 10:
                    turn_v(c, u - 6)
                if c == 2 and u == 11:
                    pe.wait_ge(n_v, 8)
                    for k in range(4):
                        mm = pe.transpose(ps[7][:, 120 * k:120 * (k + 1)], rows[0:120, P * k:P * (k + 1)],
                                          cst[0:120, C_ID:C_ID + 120])
                    mm.then_inc(m_buf, 1)
                for stage in CORE.get(u, "").split():
                    p = int(stage[1])
                    if stage[0] == "K":
                        keys_scores(c, p)
                    elif stage[0] == "O":
                        output(c, p)
                    elif stage[0] == "Q":
                        square_sum(c, p)
                    elif 3 * c + p < 8:
                        update(c, p)
            pe.wait_ge(m_x, KT * NC - 1)
            ffn(1, W_F2, 0, 6, False, True, False)
            with pe.Fori(1, NB - 1) as b:
                ffn(1, W_F2, b, 6, False, False, False)
            ffn(1, W_F2, NB - 1, 6, False, False, True)
            for t in range(3, 9):
                final_turn(t)

        @block.scalar
        def _(act):
            step = Steps(act, s_acts)

            def split_hi(n, slot, dst):
                if isinstance(n, int):
                    act.wait_ge(s_ws[slot], 16 * (n // NWS + 1))
                else:
                    act.wait_ge(s_ws[slot], n[0] * 32 + 16 * (n[1] // NWS + 1))
                act.activation(dst, ws[:, slot, :], ACT.Copy).then_inc(s_whi, 1)

            def norm_squares(q, c, k_from=0, k_to=KT):
                n = CHN[c]
                for k in range(k_from, k_to):
                    depth = 2 if q < 3 else 4
                    if k >= depth or 0 < q < 3:
                        act.wait_ge(n_add, KT * q + k - depth + 1)
                    elif q:
                        act.wait_ge(n_lo, KT * q)
                    act.activation(square(q, k)[:, 0:n], xT[:, k, CH0[c]:CH0[c] + n], ACT.Square).then_inc(n_sq, 1)

            def norm_rsqrt(q, c):
                n = CHN[c]
                act.wait_ge(n_ss, q + 1)
                if 0 < q < 3:
                    act.wait_ge(n_v, q)
                act.activation(tb(0)[:, 0:n], norm_bank(q)[:, 0:n], ACT.Ln, scale=1.0 / D, bias=EPS).then_inc(n_ln, 1)
                act.wait_ge(n_ln, q + 1)
                act.activation(tb(1)[:, 0:n], tb(0)[:, 0:n], ACT.Exp, scale=-0.5).then_inc(n_y, 1)

            def norm_high(q, c, k_from, k_to):
                n = CHN[c]
                sh = ada[:, (0, 3 * KT, 6 * KT)[q // 3]:(KT, 4 * KT, 7 * KT)[q // 3], :]
                m = n if c < 2 else LASTP
                for k in range(k_from, k_to):
                    act.wait_ge(n_yk, KT * q + k + 1)
                    ins = act.activation(hh[:, k, CH0[c]:CH0[c] + m], tb(3 + k % 2)[:, 0:m], ACT.Identity, bias=sh[:, k, 0:1])
                    if c == 2:
                        ins = act.activation(hh[:, k, SEQ:TOK], tb(3 + k % 2)[:, m:n], ACT.Copy)
                    ins.then_inc(n_hi, 1)

            def norm(q, c):
                norm_squares(q, c)
                norm_rsqrt(q, c)
                norm_high(q, c, 0, KT)

            def ffn(which, base, b, first, last):
                for u in range(3 * FB):
                    f, c = unit_of(u, first or (which == 0 and last))
                    n = CHN[c]
                    act.wait_ge(s_up[which], b * 6 + (u + 1))
                    if not (first and u == 0):
                        act.wait_ge(s_a[which], b * 6 + u)
                    act.activation(tb(6)[:, 0:n], ps[2 * (u % 2)][:, 0:n], ACT.Silu).then_inc(s_silu[which], 1)
                    act.wait_ge(s_a[which], b * 6 + (u + 1))
                    act.activation(ah[:, f, CH0[c]:CH0[c] + n], tb(7)[:, 0:n], ACT.Copy).then_inc(s_ahi[which], 1)
                    if u == 0:
                        if not first:
                            act.wait_ge(s_down[which], b * 24)
                        for t in (4, 5):
                            split_hi((b, base + t) if not isinstance(b, int) else b * 6 + base + t, t % 3, wh[:, t, :])
                    if first and u == 0:
                        norm_rsqrt(6 * which + 2, 2)
                    if first and u < 3:
                        norm_high(6 * which + 2, 2, LATE[u], LATE[u + 1])
                    if last and which == 0 and u == 3:
                        act.wait_ge(s_xacc[0], 24 * (NB - 1) + KT)
                        norm_squares(3, 0)
                    if last and which == 0 and u == 4:
                        norm_rsqrt(3, 0)
                        norm_high(3, 0, 0, 2)
                    if u == (4 if first else 3) and not last:
                        for t in (0, 1):
                            split_hi((b, base + 6 + t) if not isinstance(b, int) else b * 6 + base + 6 + t, t % 3, wh[:, t, :])
                if not last:
                    for t in (2, 3):
                        split_hi((b, base + 6 + t) if not isinstance(b, int) else b * 6 + base + 6 + t, t % 3, wh[:, t, :])

            act.dma_start(cin[0:1, :], i["c_prompt"]).then_inc(s_small, 16)
            act.dma_start(cin[1:9, :], i["c_sample"]).then_inc(s_small, 16)
            for name, r, n in (("b_ada", R_BADA, 72), ("ln_ffn1", R_LN1, 8), ("ln_mix", R_LNM, 8), ("ln_ffn2", R_LN2, 8),
                               ("b_gk2", R_BGK, 2), ("pool_scale", R_PS, 4), ("gla_norm", R_GN, 1)):
                act.dma_start(vin[r:r + n, :], i[name].rearrange("a (r p) -> (a r) p", p=P)).then_inc(s_small, 16)
            act.wait_ge(s_tr, 2 * NX + 2)
            act.wait_ge(s_cs, 1)
            act.activation(csT[:, :, 0:9], ps[1][:, 0:9 * KT].rearrange("p (k s) -> p k s", s=9), ACT.Silu).then_inc(s_cs, 1)
            act.wait_ge(s_trev, 2 * NX)
            norm_squares(0, 0)
            norm_rsqrt(0, 0)
            norm_squares(1, 1)
            act.wait_ge(s_apf, 4)
            norm_high(0, 0, 0, KT)
            act.wait_ge(s_tr, 2 + 2 * NX)
            for t in range(4):
                split_hi(t, t % NWS, wh[:, t, :])
                if t == 2:
                    norm_squares(2, 2)
            norm_rsqrt(1, 1)
            norm_high(1, 1, 0, KT)
            act.wait_ge(n_add, 3 * KT)
            ffn(0, W_F1, 0, True, False)
            with act.Fori(1, NB - 1) as b:
                ffn(0, W_F1, b, False, False)
            ffn(0, W_F1, NB - 1, False, True)

            norm_high(3, 0, 2, KT)
            act.wait_ge(s_down[0], 24 * NB)
            split_hi(W_MIX, W_MIX % NWS, mwh[:, 0, :])
            split_hi(W_MIX + 1, (W_MIX + 1) % NWS, mwh[:, 1, :])

            def core_squares(c, p):
                t = 3 * c + p
                w = NS if t == 8 else P
                act.wait_ge(g_o, t + 1)
                if p == 0:
                    act.wait_ge(n_lo, KT * (LAST_NORM[c] + 1))
                else:
                    act.wait_ge(g_ss, t)
                for a in range(2):
                    ins = act.activation(tmp[:, 2 * w * a:2 * w * (a + 1)].rearrange("p (j n) -> p j n", j=2),
                                         ps[5 + a][:, 0:2 * P].rearrange("p (j n) -> p j n", j=2)[:, :, 0:w], ACT.Square)
                ins.then_inc(g_sq, 1)

            def core_rsqrt(c, p):
                t = 3 * c + p
                w = NS if t == 8 else P
                act.wait_ge(g_ss, t + 1)
                if t:
                    act.wait_ge(g_y, t)
                    act.wait_ge(g_f, t)
                act.activation(tmp[:, 512:512 + 4 * w], ps[7][:, 0:4 * w], ACT.Ln, scale=1.0 / DV, bias=EPS).then_inc(g_ln, 1)
                act.wait_ge(g_ln, t + 1)
                act.activation(tmp[:, 1024:1024 + 4 * w], tmp[:, 512:512 + 4 * w], ACT.Exp, scale=-0.5).then_inc(g_y, 1)

            def after(c, g):
                sl = slice(CH0[c], CH0[c] + CHN[c])
                act.wait_ge(m_z, 4 * c + g + 1)
                act.activation(hh[:, g, sl], ps[3 + g % 2][:, 0:CHN[c]], ACT.Copy, scale=vec[:, R_PS + g:R_PS + g + 1]).then_inc(m_zh, 1)
                if g == 0:
                    core_rsqrt(c, 2)
                if g == 2:
                    act.wait_ge(g_f, 3 * c + 3)
                    act.activation(hh[:, 4:8, sl], og[:, :, 0:CHN[c]], ACT.Copy).then_inc(g_hi, 1)

            for g, (kind, c, u) in enumerate(UNITS):
                if (kind, c, u) == ("w", 2, 0):
                    for k in range(4):
                        after(2, k)
                n = CHN[c]
                act.wait_ge(m_unit, g + 1)
                if g + 2 < NU:
                    split_hi(W_MIX + g + 2, (W_MIX + g + 2) % NWS, mwh[:, g % 2, :])
                elif g + 2 == NU:
                    act.wait_ge(m_ust, 32)
                    act.wait_ge(g_s0, NSEQ)
                    act.wait_ge(m_st, 64)
                    for t in range(4):
                        split_hi(W_F2 + t, (W_F2 + t) % NWS, wh[:, t, :])
                if kind == "p":
                    name, j, _ = PROJ[u]
                    bank = ps[g % RING]
                    if name == "glr":
                        if c:
                            act.wait_ge(m_vt, 4 * c)
                        act.activation(glr[0:16, 0:n], bank[0:16, 0:n], ACT.Copy).then_inc(m_ev, 1)
                    elif name == "k":
                        act.activation(ks[:, j, 0:n], bank[:, 0:n], ACT.Copy).then_inc(m_ev, 1)
                    elif name == "q":
                        act.activation(qs[:, j, 0:n], bank[:, 0:n], ACT.Copy).then_inc(m_ev, 1)
                    elif name == "v":
                        if j == 0:
                            act.wait_ge(m_gk, 2 * (c + 1))
                        else:
                            act.wait_ge(m_vt, 4 * c + j)
                        act.activation(vtmp[:, 0:n], bank[:, 0:n], ACT.Copy).then_inc(m_ev, 1)
                    elif name == "u":
                        m = n if c < 2 else LASTP
                        if c:
                            act.wait_ge(m_z, 4 * c)
                        ins = act.activation(E[:, j, HALO:HALO + m], bank[:, 0:m], ACT.Copy)
                        if c == 2:
                            act.activation(sample_u(j), seqs(bank[:, m:n]), ACT.Copy)
                            act.wait_ge(m_vt, 4 * (c + 1))
                            ins = act.activation(vtmp[:, NS * j:NS * (j + 1)], bank[:, m:n], ACT.Copy)
                        ins.then_inc(m_ev, 1)
                    else:
                        if c:
                            act.wait_ge(g_lo, c)
                        act.activation(og[:, j, 0:n], bank[:, 0:n], ACT.Silu).then_inc(m_ev, 1)
                for q, (nc_, s_sq, s_sum, s_hi) in NORMS.items():
                    if (kind, c, u) in s_sq:
                        k, per = s_sq.index((kind, c, u)), KT // len(s_sq)
                        if k == 0:
                            if q < 6:
                                act.wait_ge(s_xacc[0], 24 * (NB - 1) + KT * (nc_ + 1))
                            else:
                                act.wait_ge(m_x, KT * (nc_ + 1))
                            if q in (5, 6):
                                act.wait_ge(g_f, 3 * (q - 4))
                        norm_squares(q, nc_, per * k, per * (k + 1))
                    if (kind, c, u) == s_sum:
                        norm_rsqrt(q, nc_)
                    if (kind, c, u) in s_hi:
                        k = s_hi.index((kind, c, u))
                        norm_high(q, nc_, 2 * k, 2 * k + 2)
                if kind == "w":
                    continue
                if c and u < 4:
                    after(c - 1, u)
                if u == 4:
                    act.wait_ge(m_gk, 2 * (c + 1))
                    for j in range(2):
                        ins = act.activation(t1[:, j, 0:n], ps[5 + j][:, 0:n], ACT.Abs, bias=vec[:, R_BGK + j:R_BGK + j + 1])
                    step(ins)
                    step(act.activation(t1[:, :, 0:n], t1[:, :, 0:n], ACT.Exp, scale=-1.0))
                    act.activation(t1[:, :, 0:n], t1[:, :, 0:n], ACT.Ln, bias=1.0).then_inc(m_pa, 1)
                if u == 5:
                    act.wait_ge(m_pd, 4 * c + 1)
                    act.activation(t1[:, :, 0:n], bs[:, :, 0:n], ACT.Exp, scale=1.0 / 16).then_inc(m_pa, 1)
                if u == 6:
                    act.wait_ge(m_pd, 4 * c + 2)
                    act.activation(t1[:, :, 0:n], bs[:, :, 0:n], ACT.Exp, scale=-1.0 / 16)
                    act.activation(dec[:, :, :], bl[:, :, :], ACT.Exp, scale=1.0 / 16).then_inc(m_pa, 1)
                if u == 7:
                    act.wait_ge(m_pd, 4 * c + 3)
                    act.activation(bs[:, :, 0:n], bs[:, :, 0:n], ACT.Exp, scale=1.0 / 16).then_inc(m_pa, 1)
                if u in (12, 14, 16):
                    core_squares(c, (u - 12) // 2)
                if u in (13, 15):
                    core_rsqrt(c, (u - 13) // 2)
            act.wait_ge(m_x, KT * NC)
            norm_squares(8, 2)
            ffn(1, W_F2, 0, True, False)
            with act.Fori(1, NB - 1) as b:
                ffn(1, W_F2, b, False, False)
            ffn(1, W_F2, NB - 1, False, True)
            for t in range(9):
                w = P if t < 8 else NS
                act.wait_ge(s_ft, t + 1)
                for a in range(2):
                    step(act.activation(tmp[0:w, 0:512], turned(t, a)[0:w, :], ACT.Square, accum_out=rsf[0:w, t, a:a + 1]))
                step(act.activation(rsf[0:w, t, 2:3], rsf[0:w, t, 0:1], ACT.Identity, bias=rsf[0:w, t, 1:2]))
                act.activation(rsf[0:w, t, 3:4], rsf[0:w, t, 2:3], ACT.Sqrt, scale=1.0 / D, bias=EPS).then_inc(s_fy, 1)

        @block.gpsimd
        def _(gp):
            gp.memset(csT[:, :, :], 0.0).then_inc(s_cs, 1)
            gp.memset(ones[:, :], 1.0).then_inc(s_ones, 1)

            def norm(q, c):
                n = CHN[c]
                if q:
                    gp.wait_ge(n_ss, q)
                for k in range(KT):
                    gp.wait_ge(n_sq, KT * q + k + 1)
                    if k == 0:
                        gp.tensor_copy(tb(2)[:, 0:n], square(q, 0)[:, 0:n]).then_inc(n_add, 1)
                    else:
                        gp.wait_ge(n_add, KT * q + k)
                        gp.tensor_tensor(tb(2)[:, 0:n], tb(2)[:, 0:n], square(q, k)[:, 0:n], ALU.add).then_inc(n_add, 1)

            for q in range(4):
                norm(q, q % 3)
            gp.wait_ge(s_down[0], 24 * NB)
            gp.wait_ge(s_act[0], 6 * NB)
            gp.wait_ge(m_unit, 1)
            gp.memset(attS[:, :, :], 0.0).then_inc(m_init, 1)
            gp.memset(S[:, 0, :, :], 0.0).then_inc(m_init, 1)
            step = Steps(gp, s_pool)
            step(gp.memset(halo[:, :, :], 0.0))
            for c in range(NC):
                for q in ((4,), (5,), (6, 7))[c]:
                    norm(q, NORMS[q][0])
                m = CHN[c] if c < 2 else LASTP
                W = HALO + m if c < 2 else EW
                if c == 2:
                    gp.wait_ge(m_bufc, 1)
                for g in range(4):
                    gp.wait_ge(m_ev, NPROJ * c + IDX["u", g] + 1)
                    step(gp.tensor_copy(E[:, g, 0:HALO], halo[:, g, :]))
                    step(gp.tensor_copy(halo[:, g, :], E[:, g, m:m + HALO]))
                    if g or c:
                        gp.wait_ge(m_p, 4 * c + g)
                    lo = 0
                    for k in range(g + 1):
                        dst = (TA, TB)[k % 2]
                        src = E[:, g, :] if k == 0 else (TB, TA)[k % 2][:, :]
                        lo += 1 << k
                        ins = gp.tensor_tensor(dst[:, lo:W], src[:, lo:W], src[:, lo - (1 << k):W - (1 << k)], ALU.add)
                        if k < g or c == 0:
                            step(ins)
                    if c == 0:
                        ins = gp.tensor_tensor(dst[:, HALO:2 * HALO], dst[:, HALO:2 * HALO],
                                               cst[:, C_RATIO + HALO * g:C_RATIO + HALO * (g + 1)], ALU.mult)
                    ins.then_inc(m_win, 1)
            norm(8, 2)

        @block.vector
        def _(dve):
            step = Steps(dve, s_dve)

            def norm_coef(q, scale_vec, row):
                step(dve.scalar_tensor_tensor(out=coef[:, q, :, :], in0=ada[:, scale_vec * KT:(scale_vec + 1) * KT, :], scalar=1.0,
                                              in1=vec[:, row:row + KT].unsqueeze(2).broadcast_to([P, KT, 9]), op0=ALU.add, op1=ALU.mult))

            def half_gain(v):
                a = ada[:, v * KT:(v + 1) * KT, :]
                step(dve.tensor_scalar(a, a, 0.5, None, ALU.mult))

            def split_lo(n, slot, dst, high):
                dve.wait_ge(s_whi, n + 1)
                dve.tensor_tensor(dst, ws[:, slot, :], high.bitcast(F32), ALU.subtract).then_inc(s_wsp, 1)

            def norm(q, c, part):
                n = CHN[c]
                m = n if c < 2 else LASTP
                k0 = (0, 3 * KT, 6 * KT)[q // 3]
                sh, co = ada[:, k0:k0 + KT, :], coef[:, q // 3, :, :]
                v, t3, R = tb(3)[:, 0:n], tb(4)[:, 0:n], tb(5)[:, 0:n]
                if part == 0:
                    norm_factor(q, n, v, t3, R)
                    return

                def scaled(k):
                    yb = tb(3 + k % 2)
                    ins = dve.scalar_tensor_tensor(out=yb[:, 0:m], in0=xT[:, k, CH0[c]:CH0[c] + m], scalar=co[:, k, 0:1],
                                                   in1=R[:, 0:m], op0=ALU.mult, op1=ALU.mult)
                    if c == 2:
                        step(dve.tensor_tensor(yb[:, m:n], xT[:, k, SEQ:TOK], R[:, m:n], ALU.mult))
                        step(dve.tensor_tensor(seqs(yb[:, m:n]), seqs(yb[:, m:n]),
                                               co[:, k, 1:9].unsqueeze(2).broadcast_to([P, NSEQ, TSEQ]), ALU.mult))
                        ins = dve.tensor_tensor(seqs(yb[:, m:n]), seqs(yb[:, m:n]),
                                                sh[:, k, 1:9].unsqueeze(2).broadcast_to([P, NSEQ, TSEQ]), ALU.add)
                    ins.then_inc(n_yk, 1)

                if part == 1:
                    scaled(0)
                    return
                k = part - 2
                if k + 1 < KT:
                    if k:
                        dve.wait_ge(n_lo, KT * q + k)
                    scaled(k + 1)
                yb = tb(3 + k % 2)
                dve.wait_ge(n_hi, KT * q + k + 1)
                ins = dve.scalar_tensor_tensor(out=hl[:, k, CH0[c]:CH0[c] + m], in0=yb[:, 0:m], scalar=sh[:, k, 0:1],
                                               in1=hh[:, k, CH0[c]:CH0[c] + m].bitcast(F32), op0=ALU.add, op1=ALU.subtract)
                if c == 2:
                    ins = dve.tensor_tensor(hl[:, k, SEQ:TOK], yb[:, m:n], hh[:, k, SEQ:TOK].bitcast(F32), ALU.subtract)
                ins.then_inc(n_lo, 1)

            def norm_all(q, c):
                for part in range(10):
                    norm(q, c, part)

            def norm_factor(q, n, v, t3, R):
                dve.wait_ge(n_ln, q + 1)
                if q:
                    dve.wait_ge(n_lo, KT * q)
                y = tb(1)[:, 0:n]
                dve.tensor_scalar(v, norm_bank(q)[:, 0:n], 1.0 / D, EPS, ALU.mult, ALU.add)
                dve.wait_ge(n_y, q + 1)
                step(dve.tensor_tensor(t3, y, y, ALU.mult))
                step(dve.scalar_tensor_tensor(out=t3, in0=t3, scalar=-0.5, in1=v, op0=ALU.mult, op1=ALU.mult))
                dve.scalar_tensor_tensor(out=R, in0=t3, scalar=1.5, in1=y, op0=ALU.add, op1=ALU.mult).then_inc(n_v, 1)
                dve.wait_ge(n_v, q + 1)

            def add_residual(bank, k, c, gain, done):
                m = CHN[c] if c < 2 else LASTP
                xs = xT[:, k, CH0[c]:CH0[c] + m]
                ins = dve.scalar_tensor_tensor(out=xs, in0=bank[:, 0:m], scalar=ada[:, gain + k, 0:1], in1=xs, op0=ALU.mult, op1=ALU.add)
                if c == 2:
                    t = tb(7)[:, NS * (k % 2):NS * (k % 2 + 1)]
                    step(dve.tensor_tensor(seqs(t), seqs(bank[:, m:m + NS]),
                                           ada[:, gain + k, 1:9].unsqueeze(2).broadcast_to([P, NSEQ, TSEQ]), ALU.mult))
                    ins = dve.tensor_tensor(xT[:, k, SEQ:TOK], xT[:, k, SEQ:TOK], t, ALU.add)
                ins.then_inc(done, 1)

            def ada_sums(bank):
                dve.tensor_copy(aev[:, :], bank[:, :]).then_inc(s_aevc, 1)

            def ada_store(n, bank):
                dve.wait_ge(s_asel, n + 1)
                dve.tensor_tensor(ada[:, bass.ds(n * 4, 4), :], bank[:, 0:40].rearrange("p (a s) -> p a s", s=10)[:, :, 0:9],
                                  vec[:, bass.ds(n * 4, 4)].unsqueeze(2).broadcast_to([P, 4, 9]), ALU.add).then_inc(s_ada, 1)

            def ffn(which, base, b, gain, first, last, adas):
                if not first:
                    dve.wait_ge(s_xacc[which], b * 24)
                by_chunk = first or (which == 0 and last)

                def up(u):
                    f, c = unit_of(u, by_chunk)
                    n = CHN[c]
                    dve.wait_ge(s_silu[which], b * 6 + (u + 1))
                    if not (first and u == 0):
                        dve.wait_ge(s_act[which], b * 6 + u)
                    dve.tensor_tensor(tb(7)[:, 0:n], tb(6)[:, 0:n], ps[2 * (u % 2) + 1][:, 0:n], ALU.mult).then_inc(s_a[which], 1)
                    dve.wait_ge(s_ahi[which], b * 6 + (u + 1))
                    dve.tensor_tensor(al[:, f, CH0[c]:CH0[c] + n], tb(7)[:, 0:n], ah[:, f, CH0[c]:CH0[c] + n].bitcast(F32),
                                      ALU.subtract).then_inc(s_act[which], 1)
                    if u == 0:
                        for t in (4, 5):
                            split_lo(b * 6 + (base + t), t % 3, wl[:, t, :], wh[:, t, :])
                    if first and u < 3:
                        for part in range(LATE[u] + 2 * (u > 0), LATE[u + 1] + 2):
                            norm(6 * which + 2, 2, part)
                    if u == (4 if first else 3) and not last:
                        for t in (0, 1):
                            split_lo(b * 6 + (base + 6 + t), t % 3, wl[:, t, :], wh[:, t, :])
                    if u == 4 and adas:
                        dve.wait_ge(s_apc, b * KT + KT)
                        ada_sums(ps[7])

                def down(c):
                    for k in range(KT):
                        n = KT * c + k
                        dve.wait_ge(s_down[which], b * 24 + (n + 1))
                        add_residual(ps[4 + n % 3], k, c, gain, s_xacc[which])
                        if not last and n in (3, 6):
                            t = n // 3 + 1
                            split_lo(b * 6 + (base + 6 + t), t % 3, wl[:, t, :], wh[:, t, :])
                        if last and which == 0 and 16 <= n < 22:
                            norm(3, 0, n - 12)
                        if last and which == 0 and n == 23:
                            split_lo(W_MIX, W_MIX % NWS, mwl[:, 0, :], mwh[:, 0, :])
                        if last and which == 1 and n in (17, 20, 23):
                            final((n - 17) // 3)
                        if adas and n == (11 if last else KT - 1):
                            ada_store(b + AU_FIRST, ps[7])
                    if adas and last and c == 1:
                        dve.wait_ge(s_ada, NAU)
                        norm_coef(1, 4, R_LNM)
                        norm_coef(2, 7, R_LN2)
                        half_gain(8)
                        dve.wait_ge(s_xacc[0], 24 * (NB - 1) + KT)
                        for part in range(4):
                            norm(3, 0, part)

                for what in block_order(which, last):
                    if what >= 0:
                        up(what)
                    else:
                        down(-1 - what)

            def final(t):
                if t == 0:
                    dve.wait_ge(s_lnf, 16)
                w = P if t < 8 else NS
                r = rsf[0:w, t, :]
                dve.wait_ge(s_fy, t + 1)
                step(dve.reciprocal(r[:, 4:5], r[:, 3:4]))
                step(dve.tensor_scalar(r[:, 5:6], r[:, 2:3], 1.0 / D, EPS, ALU.mult, ALU.add))
                step(dve.tensor_tensor(r[:, 6:7], r[:, 4:5], r[:, 4:5], ALU.mult))
                step(dve.scalar_tensor_tensor(out=r[:, 6:7], in0=r[:, 6:7], scalar=-0.5, in1=r[:, 5:6], op0=ALU.mult, op1=ALU.mult))
                step(dve.scalar_tensor_tensor(out=r[:, 7:8], in0=r[:, 6:7], scalar=1.5, in1=r[:, 4:5], op0=ALU.add, op1=ALU.mult))
                if t >= NYST:
                    dve.wait_ge(s_out[t % NYST], 16 * (t // NYST))
                for a in range(2):
                    ins = dve.scalar_tensor_tensor(out=yst[0:w, t % NYST, 512 * a:512 * (a + 1)], in0=turned(t, a)[0:w, :],
                                                   scalar=r[:, 7:8], in1=lnf[0:w, 512 * a:512 * (a + 1)], op0=ALU.mult, op1=ALU.mult)
                ins.then_inc(s_fo, 1)

            def ffn_all(which, base, gain, adas):
                ffn(which, base, 0, gain, True, False, adas)
                with dve.Fori(1, NB - 1) as b:
                    step.loop(b - 1, KT)
                    ffn(which, base, b, gain, False, False, adas)
                step.end_loop(NB - 2)
                ffn(which, base, NB - 1, gain, False, True, adas)


            def keys_scores(c, p):
                t = 3 * c + p
                w = NS if t == 8 else P
                dve.wait_ge(g_at, t + 1)
                if t:
                    dve.wait_ge(g_u, 2 * t)
                    dve.wait_ge(g_o, t)
                dve.wait_ge(m_init, 2)
                for j in range(2):
                    dve.tensor_copy(kdT[0:w, P * j:P * (j + 1)], ps[3 + j][0:w, 3 * P:4 * P])
                if t == 8:
                    step(dve.memset(attS[0:NS, :, 0:NS], 0.0))
                mask = C_SM if t == 8 else C_CM
                for a in range(w // GC):
                    r = slice(GC * a, GC * (a + 1))
                    for h2 in range(2):
                        ins = dve.copy_predicated(attS[r, h2:4:2, r],
                                                  cst[r, mask:mask + GC].bitcast(U32).unsqueeze(1).broadcast_to([GC, 2, GC]),
                                                  ps[3 + h2][r, 0:2 * GC].rearrange("p (j n) -> p j n", j=2))
                ins.then_inc(g_am, 1)

            def states(c, p):
                for a in range(2):
                    g = 2 * (3 * c + p) + a
                    dve.wait_ge(g_u, g + 1)
                    if g:
                        dve.wait_ge(g_s, g)
                    if g >= 2:
                        dve.wait_ge(g_o, g // 2)
                    for j in range(2):
                        ins = dve.scalar_tensor_tensor(out=S[:, (g + 1) % 3, j, :], in0=S[:, g % 3, j, :],
                                                       scalar=dec[:, j, 2 * p + a:2 * p + a + 1],
                                                       in1=ps[3 + a][:, P * (1 + j):P * (2 + j)], op0=ALU.mult, op1=ALU.add)
                    ins.then_inc(g_s, 1)

            def gated(c, p):
                t = 3 * c + p
                w = NS if t == 8 else P
                dve.wait_ge(g_sq, t + 1)
                dve.wait_ge(m_ev, NPROJ * c + IDX["og", 3] + 1)
                for h2 in range(2):
                    gate = og[:, h2:4:2, P * p:P * p + w]
                    ins = dve.scalar_tensor_tensor(out=gate, in0=ps[5 + h2][:, 0:2 * P].rearrange("p (j n) -> p j n", j=2)[:, :, 0:w],
                                                   scalar=vec[:, R_GN:R_GN + 1], in1=gate, op0=ALU.mult, op1=ALU.mult)
                ins.then_inc(g_w, 1)

            def normed(c, p):
                t = 3 * c + p
                w = NS if t == 8 else P
                dve.wait_ge(g_ln, t + 1)
                if t:
                    dve.wait_ge(g_f, t)
                if p == 0:
                    dve.wait_ge(n_lo, KT * (LAST_NORM[c] + 1))
                q4 = 4 * w
                V, Y, T3, R = (tmp[:, b:b + q4] for b in (1536, 1024, 2048, 2560))
                dve.tensor_scalar(V, ps[7][:, 0:q4], 1.0 / DV, EPS, ALU.mult, ALU.add)
                dve.wait_ge(g_y, t + 1)
                step(dve.tensor_tensor(T3, Y, Y, ALU.mult))
                step(dve.scalar_tensor_tensor(out=T3, in0=T3, scalar=-0.5, in1=V, op0=ALU.mult, op1=ALU.mult))
                step(dve.scalar_tensor_tensor(out=R, in0=T3, scalar=1.5, in1=Y, op0=ALU.add, op1=ALU.mult))
                dve.wait_ge(g_w, t + 1)
                for h2 in range(2):
                    gate = og[:, h2:4:2, P * p:P * p + w]
                    ins = dve.tensor_tensor(gate, R[:, 2 * w * h2:2 * w * (h2 + 1)].rearrange("p (j n) -> p j n", j=2), gate, ALU.mult)
                ins.then_inc(g_f, 1)

            def chunks(tensor, c, a):
                n = CHN[c]
                m = n if c < 2 else LASTP
                if a == 0:
                    return tensor[:, :, 0:m].rearrange("p j (c t) -> p j c t", t=GC)
                return tensor[:, :, m:n].rearrange("p j (c t) -> p j c t", t=TSEQ)

            def log_decays(c):
                n = CHN[c]
                m = n if c < 2 else LASTP
                nc_ = m // GC
                dve.wait_ge(m_pa, 4 * c + 1)
                for j in range(2):
                    ins = dve.tensor_scalar(bs[:, j, 0:n], ps[5 + j][:, 0:n], vec[:, R_BGK + j:R_BGK + j + 1], 0.0, ALU.add, ALU.min)
                    ins.then_inc(m_gkr, 1)
                dve.wait_ge(m_gkr, 2 * (c + 1))
                step(dve.tensor_tensor(bs[:, :, 0:n], bs[:, :, 0:n], t1[:, :, 0:n], ALU.subtract))
                for j in range(2):
                    ins = dve.tensor_tensor_scan(bs[:, j, 0:m], cst[:, C_RM:C_RM + m], bs[:, j, 0:m], 0.0, ALU.mult, ALU.add)
                    if c == 2:
                        ins = dve.tensor_tensor_scan(bs[:, j, m:n], cst[:, C_RM + CMAX:C_RM + CMAX + NS], bs[:, j, m:n],
                                                     0.0, ALU.mult, ALU.add)
                step(ins)
                ins = dve.tensor_copy(bl[:, :, 0:nc_], chunks(bs, c, 0)[:, :, :, GC - 1])
                if c == 2:
                    ins = dve.tensor_copy(bl[:, :, nc_:nc_ + NSEQ], chunks(bs, c, 1)[:, :, :, TSEQ - 1])
                elif c == 0:
                    step(dve.memset(bl[:, :, nc_:12], 0.0))
                    ins = dve.tensor_copy(bl[:, :, 0:nc_], chunks(bs, c, 0)[:, :, :, GC - 1])
                ins.then_inc(m_pd, 1)

            def pooled(c, g):
                m = CHN[c] if c < 2 else LASTP
                dve.wait_ge(m_win, 4 * c + g + 1)
                W = HALO + m if c < 2 else EW
                T = (TA, TB)[g % 2]
                dve.scalar_tensor_tensor(out=E[:, g, HALO:W], in0=T[:, HALO:W], scalar=1.0 / PW[g], in1=E[:, g, HALO:W],
                                         op0=ALU.mult, op1=ALU.subtract).then_inc(m_p, 1)

            def after(c, g):
                sl = slice(CH0[c], CH0[c] + CHN[c])
                if g == 0:
                    pooled(c, 3)
                dve.wait_ge(m_zh, 4 * c + g + 1)
                dve.scalar_tensor_tensor(out=hl[:, g, sl], in0=ps[3 + g % 2][:, 0:CHN[c]], scalar=vec[:, R_PS + g:R_PS + g + 1],
                                         in1=hh[:, g, sl].bitcast(F32), op0=ALU.mult, op1=ALU.subtract).then_inc(m_zs, 1)
                if g == 1:
                    normed(c, 2)
                if g == 2:
                    dve.wait_ge(g_hi, c + 1)
                    dve.tensor_tensor(hl[:, 4:8, sl], og[:, :, 0:CHN[c]], hh[:, 4:8, sl].bitcast(F32), ALU.subtract).then_inc(g_lo, 1)
                if c == 2 and g == 3:
                    dve.wait_ge(m_ut, 1)
                    dve.tensor_copy(rows[0:HALO, :], ps[5][0:HALO, :]).then_inc(m_uc, 1)
                    dve.wait_ge(m_ut, 2)
                    dve.tensor_copy(rows[NS:2 * NS, :], ps[6][0:NS, :]).then_inc(m_uc, 1)
                    sample_keys(0)
                    sample_keys(1)

            def sample_keys(s):
                if s >= 2:
                    dve.wait_ge(g_su, s - 1)
                dve.tensor_scalar(kx[:, 256 * (s % 2):256 * (s % 2 + 1)], kdT[0:NS, :],
                                  cst[0:NS, C_SEQ + s:C_SEQ + s + 1], None, ALU.mult).then_inc(g_kx, 1)

            def sample_state(s):
                dve.wait_ge(g_su, s + 1)
                for j in range(2):
                    ins = dve.scalar_tensor_tensor(out=S0[:, j, s, :], in0=S0[:, j, s, :], scalar=dec[:, j, 4 + s:5 + s],
                                                   in1=ps[3 + s % 2][:, P * j:P * (j + 1)], op0=ALU.mult, op1=ALU.add)
                ins.then_inc(g_s0, 1)

            for t in range(NX):
                n = P if t < 8 else NS
                for a in range(2):
                    dve.wait_ge(s_tr, 1 + 2 * t + a)
                    dve.tensor_copy(xT[:, 4 * a:4 * a + 4, P * t:P * t + n],
                                    ps[2 + (2 * t + a) % 4][:, 0:4 * n].rearrange("p (k n) -> p k n", k=4)).then_inc(s_trev, 1)

            dve.wait_ge(s_tr, 2 * NX + 1)
            step(dve.tensor_copy(vec[:, 0:R_END], ps[0][:, 0:R_END]))
            for u in range(AU_FIRST):
                dve.wait_ge(s_apf, u + 1)
                if u:
                    dve.wait_ge(s_asel, u)
                ada_sums(ps[7 - 4 * (u % 2)])
                ada_store(u, ps[2])
                if u == 2:
                    norm(0, 0, 0)
                if u == 3:
                    dve.wait_ge(s_ada, 4)
                    norm_coef(0, 1, R_LN1)
                if u in (3, 4):
                    for part in (range(1, 7) if u == 3 else range(7, 10)):
                        norm(0, 0, part)
                for t in ((), (), (), (), (0, 1), (2,), (3,))[u]:
                    split_lo(t, t % NWS, wl[:, t, :], wh[:, t, :])
            dve.wait_ge(s_ada, AU_FIRST)
            half_gain(2)
            norm_all(1, 1)
            ffn_all(0, W_F1, 2 * KT, True)
            split_lo(W_MIX + 1, (W_MIX + 1) % NWS, mwl[:, 1, :], mwh[:, 1, :])
            dve.wait_ge(s_xacc[0], 24 * NB)
            for g, (kind, c, u) in enumerate(UNITS):
                if (kind, c, u) == ("w", 2, 0):
                    for k in range(4):
                        after(2, k)
                dve.wait_ge(m_unit, g + 1)
                if g + 2 < NU:
                    split_lo(W_MIX + g + 2, (W_MIX + g + 2) % NWS, mwl[:, g % 2, :], mwh[:, g % 2, :])
                if kind == "w":
                    add_residual(ps[g % RING], u, c, 5 * KT, m_x)
                    if c == 2 and u < NSEQ // 2:
                        for s in (2 * u, 2 * u + 1):
                            sample_state(s)
                            if s + 2 < NSEQ:
                                sample_keys(s + 2)
                if g + 2 >= NU:
                    for t in ((0, 1), (2, 3))[g + 2 - NU]:
                        split_lo(W_F2 + t, (W_F2 + t) % NWS, wl[:, t, :], wh[:, t, :])
                stages = CORE.get(u, "").split() if kind == "p" else []
                for stage in stages:
                    if stage[0] == "K":
                        keys_scores(c, int(stage[1]))
                    elif stage[0] == "U" and 3 * c + int(stage[1]) < 8:
                        states(c, int(stage[1]))
                for q, (nq, _, s_sum, s_hi) in NORMS.items():
                    if (kind, c, u) == s_sum:
                        norm(q, nq, 0)
                    if (kind, c, u) in s_hi:
                        k = s_hi.index((kind, c, u))
                        for part in range(2 * k + 2 - (k == 0), 2 * k + 4):
                            norm(q, nq, part)
                if (kind, c, u) == ("p", 0, WSTART - 1) or kind == "w" and u == 0 and c < 2:
                    log_decays(c if kind == "p" else c + 1)
                if kind == "p":
                    if c and u < 4:
                        after(c - 1, u)
                    n = CHN[c]
                    m = n if c < 2 else LASTP
                    nc_ = m // GC

                    if u == 5:
                        dve.wait_ge(m_pa, 4 * c + 2)
                        dve.wait_ge(m_ev, NPROJ * c + IDX["q", 1] + 1)
                        dve.scalar_tensor_tensor(out=qs[:, :, 0:n], in0=qs[:, :, 0:n], scalar=DK ** -0.5, in1=t1[:, :, 0:n],
                                                 op0=ALU.mult, op1=ALU.mult).then_inc(m_pd, 1)
                    if u == 6:
                        dve.wait_ge(m_pa, 4 * c + 3)
                        ins = dve.tensor_tensor(chunks(bs, c, 0), bl[:, :, 0:nc_].unsqueeze(3).broadcast_to([P, 2, nc_, GC]), chunks(bs, c, 0), ALU.subtract)
                        if c == 2:
                            ins = dve.tensor_tensor(chunks(bs, c, 1), bl[:, :, nc_:nc_ + NSEQ].unsqueeze(3).broadcast_to([P, 2, NSEQ, TSEQ]),
                                                    chunks(bs, c, 1), ALU.subtract)
                        ins.then_inc(m_pd, 1)
                    if u == 7:
                        dve.wait_ge(m_pa, 4 * c + 4)
                        step(dve.tensor_tensor(bs[:, :, 0:n], bs[:, :, 0:n], ks[:, :, 0:n], ALU.mult))
                        dve.tensor_tensor(ks[:, :, 0:n], ks[:, :, 0:n], t1[:, :, 0:n], ALU.mult).then_inc(m_pd, 1)
                    if 6 <= u < 10:
                        h = u - 6
                        dve.wait_ge(m_vt, 4 * c + h + 1)
                        full = m // P
                        src = ps[5 + h % 2]
                        ins = dve.tensor_copy(vs[:, 0:full, DV * h:DV * (h + 1)], src[:, 0:P * full].rearrange("p (t e) -> p t e", e=P))
                        if c == 2:
                            dve.memset(vs[NS:P, full, DV * h:DV * (h + 1)], 0.0)
                            ins = dve.tensor_copy(vs[0:NS, full, DV * h:DV * (h + 1)], src[0:NS, P * full:P * (full + 1)])
                        ins.then_inc(m_vc, 1)
                    for stage in stages:
                        if stage[0] == "O":
                            gated(c, int(stage[1]))
                        elif stage[0] == "Q":
                            normed(c, int(stage[1]))
                    if c == 2 and u == 11:
                        dve.wait_ge(m_buf, 1)
                        dve.wait_ge(m_z, 8)
                        for gg in range(4):
                            ins = dve.tensor_copy(sample_rows(gg)[:, :, 0:HALO],
                                                  ps[7][:, 120 * gg:120 * (gg + 1)].rearrange("p (s r) -> p s r", r=HALO))
                        ins.then_inc(m_bufc, 1)
                    if 14 <= u < NPROJ:
                        pooled(c, u - 14)
            dve.wait_ge(m_x, KT * NC)
            ffn_all(1, W_F2, 8 * KT, False)
            for t in range(3, 9):
                final(t)


_INS = ("x_prompt", "x_sample", "state_pool", "state_gla", "c_prompt", "c_sample", "ln_ffn1", "ln_mix", "ln_ffn2", "w_ada", "b_ada",
        "w_ffn1_up", "w_ffn1_down", "w_in", "w_gk2", "b_gk2", "w_pool", "pool_scale", "gla_norm", "w_out", "w_ffn2_up",
        "w_ffn2_down", "ln_final")
_LAYER = ("w_ada", "w_ffn1_up", "w_ffn1_down", "w_in", "w_gk2", "w_pool", "w_out", "w_ffn2_up", "w_ffn2_down")
_OUTS = (("y_p", (1, SEQ, D)), ("y_s", (NSEQ, TSEQ, D)), ("pool_p", (1, 1, HALO, 512)), ("gla_p", (1, 1, HEADS, DK, DV)),
         ("pool_s", (1, NSEQ, HALO, 512)), ("gla_s", (1, NSEQ, HEADS, DK, DV)))


def kernel(**inputs):
    import concourse.bacc as _bacc
    from concourse.bass_utils import run_bass_kernel_spmd as _run

    nc = _bacc.Bacc("TRN2", target_bir_lowering=False, num_devices=1)
    arrays, i, o = {}, {}, {}
    for name in _INS + ("const",):
        a = constants() if name == "const" else np.ascontiguousarray(inputs[name])
        if name in _LAYER:
            a = a[0]
        arrays[f"in_{name}"] = a
        i[name] = nc.dram_tensor(f"in_{name}", a.shape, F32, kind="ExternalInput").ap()
    for name, shape in _OUTS:
        o[name] = nc.dram_tensor(f"out_{name}", shape, F32, kind="ExternalOutput").ap()
    program(nc, i, o)
    r = _run(nc, [arrays], core_ids=[0])
    return tuple(r.results[0][f"out_{name}"] for name, _ in _OUTS)
```
